# Optimizing a Trainium2 kernel written in Bass

```python
import jax, jax.numpy as jnp
from jax import lax
import numpy as np

D_MODEL = 1024
BATCH = 1
SEQ = 512
DEPTH = 2
DEC_BATCH = 8
DEC_SEQ = 8
PAST_LEN = 2048
PAGE_SIZE = 128

HEAD_DIM = 64
N_HEADS = D_MODEL // HEAD_DIM
H_A = N_HEADS // 2
KVH_A = 2
G_A = H_A // KVH_A
H_B = N_HEADS - H_A
CMP_LEN = 32
CMP_STRIDE = 16
CMP_HIDDEN = 2 * HEAD_DIM
SEL_LEN = 64
SEL_TOP = 16
WIN_A = 512
DIL_CONFIGS = ((128, 1), (512, 4), (2048, 16))
WIN_B = 2048
D_FF = 4 * D_MODEL
BLOCK = 128
RMS_EPS = 1e-6
NEG = -1e30
FORCE = 1e9
SCALE = HEAD_DIM ** -0.5
SPLITS = (H_A * HEAD_DIM, 2 * KVH_A * HEAD_DIM, 2 * KVH_A * HEAD_DIM, 2 * KVH_A * HEAD_DIM,
          3 * H_A, H_B * HEAD_DIM, 2 * H_B * HEAD_DIM)
D_IN = sum(SPLITS)

kernel_name = 'nsa_dilated_hybrid_decode'

def _rmsnorm(x, g):
    xf = x.astype(jnp.float32)
    y = xf * lax.rsqrt(jnp.mean(xf * xf, axis=-1, keepdims=True) + RMS_EPS)
    return y.astype(x.dtype) * g

def _alibi_slopes():
    return jnp.exp2(-8.0 * jnp.arange(1, N_HEADS + 1, dtype=jnp.float32) / N_HEADS)

def _masked_softmax(s, mask):
    s = jnp.where(mask, s, NEG)
    lse = jax.nn.logsumexp(s, axis=-1, keepdims=True)
    return jnp.exp(s - lse) * mask, lse[..., 0]

def _project(h, w_in):
    B, T, _ = h.shape
    z = h @ w_in
    bounds = np.cumsum(SPLITS)[:-1].tolist()
    q_a, kv_c, kv_s, kv_w, g, q_b, kv_b = jnp.split(z, bounds, axis=-1)
    kv = lambda a, k: a.reshape(B, T, 2, k, HEAD_DIM)
    return (q_a.reshape(B, T, KVH_A, G_A, HEAD_DIM), kv(kv_c, KVH_A), kv(kv_s, KVH_A),
            kv(kv_w, KVH_A), jax.nn.sigmoid(g.reshape(B, T, H_A, 3)),
            q_b.reshape(B, T, H_B, HEAD_DIM), kv(kv_b, H_B))

def _local_attn(q, k, v, slopes, max_dist, dist_scale):
    N, L, K, G, Dh = q.shape
    nb = L // BLOCK
    n_prev = -(-max_dist // BLOCK)
    qb = q.reshape(N, nb, BLOCK, K, G, Dh)

    def band(a):
        ab = jnp.pad(a.reshape(N, nb, BLOCK, K, Dh), ((0, 0), (n_prev, 0), (0, 0), (0, 0), (0, 0)))
        return jnp.concatenate([ab[:, i:i + nb] for i in range(n_prev + 1)], axis=2)

    kb, vb = band(k), band(v)
    C = (n_prev + 1) * BLOCK
    a = jnp.arange(BLOCK)[:, None]
    c = jnp.arange(C)[None, :]
    rel = a + n_prev * BLOCK - c
    key_idx = jnp.arange(nb)[:, None, None] * BLOCK + c[None] - n_prev * BLOCK
    mask = (rel >= 0) & (rel <= max_dist) & (key_idx >= 0)
    s = jnp.einsum('nbqkgd,nbckd->nbkgqc', qb, kb).astype(jnp.float32) * SCALE
    s = s - slopes[:, :, None, None] * (rel.astype(jnp.float32) * dist_scale)
    p, lse = _masked_softmax(s, mask[None, :, None, None])
    o = jnp.einsum('nbkgqc,nbckd->nbqkgd', p.astype(v.dtype), vb)
    return o.reshape(N, L, K, G, Dh), jnp.moveaxis(lse, -1, 2).reshape(N, L, K, G)

def _compress(kv, pe, w1, w2):
    B, T, _, K, Dh = kv.shape
    n = T // CMP_STRIDE
    r = CMP_LEN // CMP_STRIDE
    n_cmp = n - r + 1
    ch = kv[:, :n * CMP_STRIDE].reshape(B, n, CMP_STRIDE, 2, K, Dh)
    parts = []
    for half in range(r):
        sl = slice(half * CMP_STRIDE, (half + 1) * CMP_STRIDE)
        pe_h = jnp.moveaxis(pe[:, sl], 0, 1)[:, :, None]
        proj = jnp.einsum('bncskd,scdh->bnskh', ch + pe_h, w1[:, sl])
        parts.append(proj[:, half:half + n_cmp])
    hid = jax.nn.silu(sum(parts))
    return jnp.einsum('bnskh,shd->bnskd', hid, w2)

def _sel_blocks(kv):
    B, T, _, K, Dh = kv.shape
    nsel = -(-T // SEL_LEN)
    kv = jnp.pad(kv, ((0, 0), (0, nsel * SEL_LEN - T), (0, 0), (0, 0), (0, 0)))
    return kv.reshape(B, nsel, SEL_LEN, 2, K, Dh).transpose(0, 4, 1, 2, 3, 5)

def _nsa_global(q, pos, kvc, blocks, slopes):
    B, Q, K, G, Dh = q.shape
    ncmp = kvc.shape[1]
    nsel = blocks.shape[2]
    end = jnp.arange(ncmp) * CMP_STRIDE + CMP_LEN - 1
    dist_c = pos[:, None] - end[None]
    s = jnp.einsum('bqkgd,bnkd->bkgqn', q, kvc[:, :, 0]).astype(jnp.float32) * SCALE
    s = s - slopes[:, :, None, None] * dist_c.astype(jnp.float32)
    p_cmp, _ = _masked_softmax(s, dist_c >= 0)
    o_cmp = jnp.einsum('bkgqn,bnkd->bqkgd', p_cmp.astype(q.dtype), kvc[:, :, 1])
    ratio = SEL_LEN // CMP_STRIDE
    offs = jnp.arange(1 - CMP_LEN // CMP_STRIDE, ratio)
    idx_c = jnp.arange(nsel)[:, None] * ratio + offs[None]
    ok = (idx_c >= 0) & (idx_c < ncmp)
    p_grp = p_cmp.sum(axis=2)
    imp = jnp.where(ok, p_grp[..., jnp.clip(idx_c, 0, ncmp - 1)], 0.0).sum(-1)
    blk = pos // SEL_LEN
    j = jnp.arange(nsel)[None]
    valid = j <= blk[:, None]
    forced = (j == 0) | (j == blk[:, None]) | (j == blk[:, None] - 1)
    score = jnp.where(valid, imp + jnp.where(forced, FORCE, 0.0), NEG)
    n_top = min(SEL_TOP, nsel)
    top_s, top_i = lax.top_k(score, n_top)
    sel_ok = top_s > NEG / 2
    kvsel = jnp.take_along_axis(blocks, top_i.reshape(B, K, Q * n_top)[..., None, None, None], axis=2)
    kvsel = kvsel.reshape(B, K, Q, n_top * SEL_LEN, 2, Dh)
    kpos5 = top_i[..., None] * SEL_LEN + jnp.arange(SEL_LEN)
    kmask = (sel_ok[..., None] & (kpos5 <= pos[:, None, None])).reshape(B, K, Q, n_top * SEL_LEN)
    dist_s = (pos[:, None] - kpos5.reshape(B, K, Q, n_top * SEL_LEN)).astype(jnp.float32)
    s = jnp.einsum('bqkgd,bkqcd->bkgqc', q, kvsel[..., 0, :]).astype(jnp.float32) * SCALE
    s = s - slopes[None, :, :, None, None] * dist_s[:, :, None]
    p_sel, _ = _masked_softmax(s, kmask[:, :, None])
    o_sel = jnp.einsum('bkgqc,bkqcd->bqkgd', p_sel.astype(q.dtype), kvsel[..., 1, :])
    return o_cmp, o_sel

def _window_sample(q, kv_all, n_buf, slopes):
    Tn, C = q.shape[1], kv_all.shape[1]
    rel = n_buf + jnp.arange(Tn)[:, None] - jnp.arange(C)[None]
    mask = (rel >= 0) & (rel < WIN_A)
    s = jnp.einsum('bqkgd,bckd->bkgqc', q, kv_all[:, :, 0]).astype(jnp.float32) * SCALE
    s = s - slopes[:, :, None, None] * rel.astype(jnp.float32)
    p, _ = _masked_softmax(s, mask)
    return jnp.einsum('bkgqc,bckd->bqkgd', p.astype(q.dtype), kv_all[:, :, 1])

def _combine_dilations(outs, lses):
    w = jax.nn.softmax(jnp.stack(lses), axis=0)
    return jnp.einsum('cbth,cbthd->bthd', w.astype(outs[0].dtype), jnp.stack(outs))

def _dilated_prompt(q, kv, slopes):
    B, S, H, Dh = q.shape
    outs, lses = [], []
    for win, dil in DIL_CONFIGS:
        L = S // dil
        Lp = -(-L // BLOCK) * BLOCK

        def sub(a):
            rest = a.shape[2:]
            a = jnp.moveaxis(a.reshape((B, L, dil) + rest), 2, 1).reshape((B * dil, L) + rest)
            return jnp.pad(a, [(0, 0), (0, Lp - L)] + [(0, 0)] * len(rest))

        kvs = sub(kv)
        o, lse = _local_attn(sub(q)[:, :, :, None], kvs[:, :, 0], kvs[:, :, 1], slopes[:, None],
                             win // dil, float(dil))
        outs.append(jnp.moveaxis(o[:, :L, :, 0].reshape(B, dil, L, H, Dh), 1, 2).reshape(B, S, H, Dh))
        lses.append(jnp.moveaxis(lse[:, :L, :, 0].reshape(B, dil, L, H), 1, 2).reshape(B, S, H))
    return _combine_dilations(outs, lses)

def _dilated_sample(q, kv_all, n_buf, slopes):
    Tn = q.shape[1]
    outs, lses = [], []
    for win, dil in DIL_CONFIGS:
        j = jnp.arange(win // dil + 1)
        idx = n_buf + jnp.arange(Tn)[:, None] - j[None] * dil
        g = kv_all[:, jnp.maximum(idx, 0)]
        s = jnp.einsum('bqhd,bqjhd->bhqj', q, g[:, :, :, 0]).astype(jnp.float32) * SCALE
        s = s - slopes[:, None, None] * (j * dil).astype(jnp.float32)
        p, lse = _masked_softmax(s, idx >= 0)
        outs.append(jnp.einsum('bhqj,bqjhd->bqhd', p.astype(q.dtype), g[:, :, :, 1]))
        lses.append(jnp.transpose(lse, (0, 2, 1)))
    return _combine_dilations(outs, lses)

def _merge(o_cmp, o_sel, o_win, gate, o_dil, w_out):
    B, T = gate.shape[:2]
    o_a = jnp.stack([o_cmp, o_sel, o_win], axis=-1).reshape(B, T, H_A, HEAD_DIM, 3)
    o_a = jnp.einsum('bthdc,bthc->bthd', o_a, gate)
    return jnp.concatenate([o_a.reshape(B, T, -1), o_dil.reshape(B, T, -1)], axis=-1) @ w_out

def _mlp(h, w_up, w_down):
    return jnp.square(jax.nn.relu(h @ w_up)) @ w_down

def _mixers_prompt(h, w_in, pe, w1, w2, w_out, slopes_a, slopes_b):
    B, S, _ = h.shape
    q_a, kv_c, kv_s, kv_w, gate, q_b, kv_b = _project(h, w_in)
    kvc = _compress(kv_c, pe, w1, w2)
    blocks = _sel_blocks(kv_s)
    nb = S // BLOCK
    qb = jnp.moveaxis(q_a.reshape(B, nb, BLOCK, KVH_A, G_A, HEAD_DIM), 1, 0)
    posb = jnp.arange(S, dtype=jnp.int32).reshape(nb, BLOCK)
    o_cmp, o_sel = lax.map(lambda qp: _nsa_global(qp[0], qp[1], kvc, blocks, slopes_a), (qb, posb))
    o_cmp = jnp.moveaxis(o_cmp, 0, 1).reshape(B, S, KVH_A, G_A, HEAD_DIM)
    o_sel = jnp.moveaxis(o_sel, 0, 1).reshape(B, S, KVH_A, G_A, HEAD_DIM)
    o_win, _ = _local_attn(q_a, kv_w[:, :, 0], kv_w[:, :, 1], slopes_a, WIN_A - 1, 1.0)
    o_dil = _dilated_prompt(q_b, kv_b, slopes_b)
    y = _merge(o_cmp, o_sel, o_win, gate, o_dil, w_out)
    return y, kv_c, kv_s, kv_w[:, S - min(WIN_A, S):], kv_b[:, S - min(WIN_B, S):]

def _mixers_sample(h, pool_cmp, pool_sel, buf_win, buf_dil, page_table, w_in, pe, w1, w2, w_out,
                   slopes_a, slopes_b):
    B, Tn, _ = h.shape
    q_a, kv_c, kv_s, kv_w, gate, q_b, kv_b = _project(h, w_in)
    past_len = page_table.shape[1] * PAGE_SIZE
    pos = past_len + jnp.arange(Tn, dtype=jnp.int32)

    def gather(pool):
        return pool[page_table].reshape((B, past_len) + pool.shape[2:])

    kvc = _compress(jnp.concatenate([gather(pool_cmp), kv_c], axis=1), pe, w1, w2)
    blocks = _sel_blocks(jnp.concatenate([gather(pool_sel), kv_s], axis=1))
    o_cmp, o_sel = _nsa_global(q_a, pos, kvc, blocks, slopes_a)
    n_win, n_dil = buf_win.shape[1], buf_dil.shape[1]
    win_all = jnp.concatenate([buf_win, kv_w], axis=1)
    o_win = _window_sample(q_a, win_all, n_win, slopes_a)
    dil_all = jnp.concatenate([buf_dil, kv_b], axis=1)
    o_dil = _dilated_sample(q_b, dil_all, n_dil, slopes_b)
    y = _merge(o_cmp, o_sel, o_win, gate, o_dil, w_out)
    return y, kv_c, kv_s, win_all[:, Tn:], dil_all[:, Tn:]

def setup_inputs(seed: int = 0) -> dict:
    key = jax.random.key(seed)
    ks = jax.random.split(key, 20)
    n_pages = PAST_LEN // PAGE_SIZE
    n_used = DEC_BATCH * n_pages
    n_pool = -(-(n_used * 5) // 4)
    nrm = jax.random.normal
    f32 = jnp.float32
    page_table = jax.random.permutation(ks[0], n_pool)[:n_used].reshape(DEC_BATCH, n_pages).astype(jnp.int32)
    return {
        'x_prompt': nrm(ks[1], (BATCH, SEQ, D_MODEL), f32),
        'x_sample': nrm(ks[2], (DEC_BATCH, DEC_SEQ, D_MODEL), f32),
        'cache_kv_cmp': nrm(ks[3], (DEPTH, n_pool, PAGE_SIZE, 2, KVH_A, HEAD_DIM), f32),
        'cache_kv_sel': nrm(ks[4], (DEPTH, n_pool, PAGE_SIZE, 2, KVH_A, HEAD_DIM), f32),
        'state_kv_win': nrm(ks[5], (DEPTH, DEC_BATCH, min(WIN_A, PAST_LEN), 2, KVH_A, HEAD_DIM), f32),
        'state_kv_dil': nrm(ks[6], (DEPTH, DEC_BATCH, min(WIN_B, PAST_LEN), 2, H_B, HEAD_DIM), f32),
        'page_table': page_table,
        'norm_attn': 1.0 + 0.02 * nrm(ks[7], (DEPTH, D_MODEL), f32),
        'w_in': nrm(ks[8], (DEPTH, D_MODEL, D_IN), f32) * D_MODEL ** -0.5,
        'cmp_pe': 0.1 * nrm(ks[9], (DEPTH, 2, CMP_LEN, HEAD_DIM), f32),
        'cmp_w1': nrm(ks[10], (DEPTH, 2, CMP_LEN, HEAD_DIM, CMP_HIDDEN), f32) * (CMP_LEN * HEAD_DIM) ** -0.5,
        'cmp_w2': nrm(ks[11], (DEPTH, 2, CMP_HIDDEN, HEAD_DIM), f32) * CMP_HIDDEN ** -0.5,
        'w_out': nrm(ks[12], (DEPTH, D_MODEL, D_MODEL), f32) * D_MODEL ** -0.5,
        'norm_mlp': 1.0 + 0.02 * nrm(ks[13], (DEPTH, D_MODEL), f32),
        'w_up': nrm(ks[14], (DEPTH, D_MODEL, D_FF), f32) * D_MODEL ** -0.5,
        'w_down': nrm(ks[15], (DEPTH, D_FF, D_MODEL), f32) * D_FF ** -0.5,
        'norm_final': 1.0 + 0.02 * nrm(ks[16], (D_MODEL,), f32),
    }

def reference(x_prompt, x_sample, cache_kv_cmp, cache_kv_sel, state_kv_win, state_kv_dil, page_table,
              norm_attn, w_in, cmp_pe, cmp_w1, cmp_w2, w_out, norm_mlp, w_up, w_down, norm_final):
    slopes = _alibi_slopes()
    slopes_a = slopes[0::2].reshape(KVH_A, G_A)
    slopes_b = slopes[1::2]
    xp, xs = x_prompt, x_sample
    cmp_p, sel_p, win_p, dil_p = [], [], [], []
    cmp_s, sel_s, win_s, dil_s = [], [], [], []
    for l in range(DEPTH):
        yp, c, s, w, d = _mixers_prompt(_rmsnorm(xp, norm_attn[l]), w_in[l], cmp_pe[l], cmp_w1[l],
                                        cmp_w2[l], w_out[l], slopes_a, slopes_b)
        cmp_p.append(c); sel_p.append(s); win_p.append(w); dil_p.append(d)
        xp = xp + yp
        xp = xp + _mlp(_rmsnorm(xp, norm_mlp[l]), w_up[l], w_down[l])
        ys, c, s, w, d = _mixers_sample(_rmsnorm(xs, norm_attn[l]), cache_kv_cmp[l], cache_kv_sel[l],
                                        state_kv_win[l], state_kv_dil[l], page_table, w_in[l], cmp_pe[l],
                                        cmp_w1[l], cmp_w2[l], w_out[l], slopes_a, slopes_b)
        cmp_s.append(c); sel_s.append(s); win_s.append(w); dil_s.append(d)
        xs = xs + ys
        xs = xs + _mlp(_rmsnorm(xs, norm_mlp[l]), w_up[l], w_down[l])
    y_prompt = _rmsnorm(xp, norm_final)
    y_sample = _rmsnorm(xs, norm_final)
    return (y_prompt, y_sample,
            jnp.stack(cmp_p), jnp.stack(sel_p), jnp.stack(win_p), jnp.stack(dil_p),
            jnp.stack(cmp_s), jnp.stack(sel_s), jnp.stack(win_s), jnp.stack(dil_s))


_drawn_inputs = setup_inputs


def setup_inputs(seed=0):
    import zlib

    import numpy as np

    out = dict(_drawn_inputs(seed))
    spreads = {}
    factors = {}
    for name, (base, spread) in spreads.items():
        noise = np.random.default_rng([zlib.crc32(name.encode()), seed]).standard_normal(out[name].shape)
        drawn = base * np.exp(spread * noise) if base else spread * noise
        out[name] = __import__('jax').numpy.asarray(drawn.astype(out[name].dtype))
    for name, factor in factors.items():
        out[name] = (out[name] * factor).astype(out[name].dtype)
    return out
```

```python
from contextlib import ExitStack

import concourse.bass as bass
import numpy as np
from concourse import mybir

F32 = mybir.dt.float32
I32 = mybir.dt.int32
ALU = mybir.AluOpType
ACT = mybir.ActivationFunctionType
X = mybir.AxisListType.X
ds = bass.ds

P = 128
D = 1024
KT = D // P
DEPTH = 2
SEQ = 512
NB, NS = 8, 8
ROWS_S = NB * NS
PAST = 2048
PAGE = 128
NPG = PAST // PAGE
POOL = 160
HD = 64
NT = 5
ROWS = [P, P, P, P, ROWS_S]
TOK = SEQ + ROWS_S
DFF = 4096
CH = 512
EPS = 1e-6
NEG = -1e30
FORCE = 1e9
WIN = 512
SCALE = HD ** -0.5
NCK_P, NCK_S = SEQ // 16, PAST // 16
BIG = 3.0e38

Z_CHUNKS = [("qa", 0, 512), ("cs", 512, 1024), ("wg", 1024, 1304), ("qb", 1304, 1816),
            ("kb", 1816, 2328), ("vb", 2328, 2840)]
Z_STORES = {"qa": 0, "cs": 2, "wg": 1, "qb": 0, "kb": 1, "vb": 1}
NZ = len(Z_CHUNKS) * NT
NZT = 5 * NT
STG = 4
W_OUT0, W_UP0, W_DN0, W_ALL = 6, 8, 16, 24

STEPS_A, STEPS_D = 24, 8
STEPS_L = 4 * STEPS_A + 4 * STEPS_D

TD_SD, TD_PTC, TD_PTW, TD_PTD, TD_PTS, TD_N = 0, 1, 2, 3, 4, 7
(SC_HID, SC_ST, SC_KTC, SC_VC, SC_S, SC_WIN, SC_IMP, SC_SEL, SC_WBD, SC_WBA, SC_N) = (
    0, 2, 3, 4, 5, 6, 8, 9, 14, 15, 16)
EX_CMP, EX_WIN, EX_DIL, EX_SEL = 1, 2, 3, 4
ND_TILES, ND_A = 13, 5


CH_L, CH_A, CH_S = 4, 4 * (2 * STEPS_A + STEPS_D), 20


def step_keys(count, m):
    if count == STEPS_A and m % 12 < 4:
        return NCK_P
    return (m % 4 + 1) * P


def shape_constants():
    f = np.float32
    slopes = np.exp2(-8.0 * np.arange(1, 17) / 16).astype(f)
    c = {}
    p = np.arange(P)[:, None]
    x = np.arange(SEQ)[None] - 384
    dist = p - x
    c["nd"] = np.where(dist >= 0, -dist, NEG).astype(f)
    n = (dist <= 128).astype(int) + (dist % 4 == 0) + (dist % 16 == 0)
    c["lnb"] = np.where(n > 0, np.log(np.maximum(n, 1)), NEG).astype(f)
    t = (np.arange(4)[None, :, None] * P + np.arange(P)[:, None, None])
    dc = t - (np.arange(32)[None, None] * 16 + 31)
    c["ndc"] = np.where((dc >= 0) & (np.arange(32) < 31), -dc, NEG).astype(f).reshape(P, 128)
    c["okrow"] = (np.arange(P)[:, None] >= 31).astype(f)
    c["mhalf"] = np.full((P, NT), -0.5, f)
    c["slopes"] = np.tile(slopes[None], (P, 1))
    c["ident"] = np.eye(P, dtype=f)
    r = np.arange(64)
    sa, ta = slopes[0::2][r // 8][:, None], (r % 8)[:, None]
    sd, td = slopes[1::2][r % 8][:, None], (r // 8)[:, None]
    pos = np.arange(PAST)[None]
    c["b_sel"] = (-sa * (PAST + ta - pos)).astype(f)
    w = np.arange(WIN)[None]
    rel = WIN + ta - w
    c["b_win"] = np.where(rel < WIN, -sa * rel, NEG).astype(f)
    k = np.arange(128)[None]
    c["b_cmp"] = np.where(k < 127, -sa * (PAST + ta - 16 * k - 31), NEG).astype(f)
    b = np.arange(NB)[None, :, None]
    b2, t2 = (r // 8)[None, None], (r % 8)[None, None]
    ok = (b == b2) & (t2 <= ta[:, :, None])
    c["nb_newa"] = -np.where(ok, -sa[:, :, None] * (ta[:, :, None] - t2), NEG).astype(f).reshape(64, 512)
    dd = td[:, :, None] - t2
    nn = 1 + (dd % 4 == 0) + (dd == 0)
    okd = (b == b2) & (dd >= 0)
    c["nb_newd"] = -np.where(okd, -sd[:, :, None] * dd + np.log(nn), NEG).astype(f).reshape(64, 512)
    d1 = np.where(k >= td, -sd * (128 + td - k), NEG)
    d4 = PAST + td - (1536 + 4 * k + td % 4)
    d2 = np.where(d4 <= 512, -sd * d4, NEG)
    c["b_dil"] = np.concatenate([d1, d2, -sd * (PAST - 16 * k)], 1).astype(f)
    forced = np.zeros((64, 33), f)
    forced[:, [0, 31, 32]] = FORCE
    c["forced"] = forced
    same = (r[:, None] // 32 == r[None] // 32) & (r[:, None] % 8 == r[None] % 8)
    c["gsum"] = same.astype(f)
    c["ones"] = np.ones((64, 128), f)
    c["tsel"] = (r[:, None] % 8 == r[None] % 8).astype(f)
    c["bsel"] = (r[:, None] // 8 == np.arange(8)[None]).astype(f)
    c["hsel"] = np.tile((r[:, None] // 8 == np.arange(8)[None])[:, None, :, None], (1, 8, 1, 3)
                        ).astype(f).reshape(64, 192)
    return c


class Count:

    def __init__(self, ctx, nc, name, per, unit=1):
        self.sem, self.per, self.unit = ctx.enter_context(nc.semaphore(name)), per, unit

    def at(self, i, k):
        return i * (self.per * self.unit) + (k * self.unit + 1)


def build(nc, i, o):
    ctx = ExitStack()
    with ctx:
        def sb(name, *shape, dt=F32):
            return ctx.enter_context(nc.sbuf_tensor(name, list(shape), dt))

        def load_sem(name, per):
            return Count(ctx, nc, name, per, 16)

        def ev(name, per):
            return Count(ctx, nc, name, per)

        const = {n: sb("c_" + n, *a.shape) for n, a in shape_constants().items()}
        ident, slopes = const["ident"], const["slopes"]
        x = sb("x", P, NT, D)
        hT = sb("hT", P, KT, TOK)
        gain = sb("gain", P, 2, KT)
        w1 = sb("w1", P, 2, 16, 128)
        w2 = sb("w2", P, 2, HD)
        pe_in = sb("pe_in", P, 2, 16)
        cbias = sb("cbias", P, 2)
        ncbias = sb("ncbias", P, 2)
        gate = sb("gate", P, NT, 24)
        sgate = sb("sgate", 64, NB, 3)
        ktcp = sb("ktcp", P, NCK_P)
        vcp = sb("vcp", NCK_P, 128)
        qd = sb("qd", P, NB, 64)
        qdb = sb("qdb", P, 4, NB, NS, 2)
        kns, knw = sb("kns", P, 64), sb("knw", P, 64)
        knb = sb("knb", P, 4, 64)
        vsm = sb("vsm", 64, 768)
        stat = sb("stat", P, 64)
        sm = sb("sm", P, 64)
        topk = sb("topk", 64, 33 * 3 + 8)
        gs = sb("gs", 64, 64)
        q_s = sb("q_s", P, 64)
        pages = sb("pages", 1, NB * NPG, dt=I32)
        ring = sb("ring", P, 2, KT * CH)
        zone = sb("zone", P, 21900)

        def part(at, *shape, rows=slice(0, P)):
            n = int(np.prod(shape))
            v = zone[rows, at:at + n]
            if len(shape) == 1:
                return v
            names = "abcd"[:len(shape)]
            return v.rearrange(f"p ({' '.join(names)}) -> p {' '.join(names)}",
                               **dict(zip(names[1:], shape[1:])))

        qaT, qbT, kbT = part(0, 4, SEQ), part(2048, 4, SEQ), part(4096, 4, SEQ)
        ksT, kwT = part(6144, SEQ), part(6656, SEQ)
        vst = part(7168, 4, 768)
        og = part(10240, 4, 128)
        W = 11328
        xn = part(W, 2, D)
        p_bias, p_biasc = part(W, 2, SEQ), part(W + 1024, 2, 128)
        p_sb = part(W + 1280, 4, SEQ)
        p_pt = part(W + 3328, 2, SEQ)
        p_q = part(W + 4352, SEQ)
        p_k = part(W + 4864, SEQ)
        stg_at = W + 8100
        stg = part(stg_at, STG, CH)
        vd = part(0, ND_TILES, CH)
        kda, kdb = part(6656, ND_A, CH), part(9216, 4, CH)
        relaid = part(W, 2048)
        xt_at = W + 2048
        biasm = part(W, 2048, rows=slice(0, 64))
        s_sel = part(W + 2048, 2112, rows=slice(0, 64))
        pts = part(W + 4160, 17, 64)
        m = W + 5248
        he, hid = part(m, 256), part(m + 256, 2, 256)
        ktc, vc = part(m + 768, 128), part(m + 896, 128)
        s_c = part(m + 1024, 128, rows=slice(0, 64))
        ptc = part(m + 1152, 64)
        s_win = part(m + 1216, 576, rows=slice(0, 64))
        st_sb = part(m + 1792, 256)
        s_d = part(m + 2048, 448, rows=slice(0, 64))
        diag = part(m + 2496, 256, rows=slice(0, 64))
        kw_sb = part(stg_at, 4, 256)
        ptw = part(stg_at + 1024, 5, 64)
        ptd = part(stg_at + 1344, 4, 64)
        wb = part(stg_at + 1600, 256)
        prod = part(stg_at + 1856, 192)
        gb, gm = diag[:, 0:192], part(m + 2048, 192, rows=slice(0, 64))
        uT = part(0, 32, TOK)
        assert m + 2752 <= stg_at and stg_at + 2048 <= 21900
        gfin = part(W + 4096, D)
        raw = ring[:, 0, :]
        rawt = raw.rearrange("p (g s k i n) -> p g s k i n", g=NPG, s=2, k=2, i=8)
        kvsel = ring[:, 1, :].rearrange("p (g f) -> p g f", g=NPG)

        bank = [ctx.enter_context(nc.psum_tensor(f"bank{n}", [P, 512], F32)) for n in range(8)]

        c_ld = load_sem("constants_loaded", 0)
        x_ld = load_sem("rows_loaded", 0)
        gain_ld, comp_ld = load_sem("gains_loaded", 2), load_sem("compression_loaded", 3)
        w_ld = [load_sem(f"weights_loaded{n}", W_ALL // 2) for n in range(2)]
        copies = load_sem("state_copied", 0)
        sq = ev("squares_summed", NT)
        rstd = ev("rstd_ready", 2)
        xn_rdy = ev("normed", NT)
        n_tr = ev("normed_transposed", 2 * NT)
        h_rdy = ev("hT_ready", 2 * NT)
        z_mm = ev("z_products", NZ)
        z_stg = ev("z_staged", NZ)
        z_tr = ev("z_transposed", NZT)
        z_te = ev("z_transposed_kept", NZT)
        z_v = ev("z_values_kept", 3 * NT)
        g_exp = ev("gates_exp", NT)
        g_rdy = ev("gates_ready", 2)
        slot_n = [0] * STG
        store_at = {}
        for n in range(NZ):
            slot_n[n % STG] += Z_STORES[Z_CHUNKS[n // NT][0]]
            store_at[n] = slot_n[n % STG]
        z_out = [load_sem(f"z_stored{s}", slot_n[s]) for s in range(STG)]
        sg_mm, sg_rdy = ev("sample_gates_product", 1), ev("sample_gates", 3)
        raw_p = load_sem("raw_prompt_loaded", 1)
        raw_ld = load_sem("raw_loaded", NPG)
        relay = ev("raw_relaid", 2)
        cleared = ev("cleared", 0)
        pb_mm, pb_rdy = ev("compress_bias_product", 1), ev("compress_bias", 2)
        ct_p, xt_p = ev("prompt_chunks_transposed", 8), ev("prompt_chunks_kept", 8)
        hid_p, hexp_p, hdone_p = ev("prompt_hidden", 2), ev("prompt_hidden_exp", 2), ev("prompt_hidden_done", 2)
        kvc_p, kvc_pk = ev("prompt_compressed", 2), ev("prompt_compressed_kept", 2)
        a_s, a_sb, a_e = ev("scores", STEPS_L), ev("scores_biased", STEPS_L), ev("probs", STEPS_L)
        a_t, a_pt, a_o = ev("probs_transposed", STEPS_L), ev("probsT_kept", STEPS_L), ev("outputs", STEPS_L)
        a_w, a_acc = ev("row_weights", 2 * STEPS_L), ev("outputs_added", STEPS_L)
        a_bias = ev("head_bias", 8)
        a_q = ev("pair_queries", 8)
        s_q = ev("batch_queries", 1)
        og_t, og_k = ev("pair_transposed", 8), ev("pair_kept", 8)
        sel_ld, win_ld = load_sem("selected_loaded", NPG), load_sem("window_loaded", 1)
        kda_ld, kdb_ld = load_sem("dilated_ka_loaded", 2), load_sem("dilated_kb_loaded", 1)
        vd_ld = load_sem("dilated_v_loaded", 1)
        td_full, td_used = ev("bank01_full", TD_N), ev("bank01_used", TD_N)
        sc_full, sc_used = ev("bank45_full", SC_N), ev("bank45_used", SC_N)
        s_hexp = ev("hidden_exp", 2)
        s_exp = ev("sample_probs", 4)
        s_max = ev("sample_max", 2)
        s_bm = ev("selection_bias", 1)
        s_mask = ev("selection_mask", 1)
        s_gs = ev("group_sums_scaled", 1)
        s_diag = ev("weights_diagonal", 2)
        oa_full, od_full = ev("sparse_out", 1), ev("dilated_out", 1)
        out_put = ev("sample_out_kept", 4)
        win_pv = ev("window_out", 1)
        kda_used = ev("dilated_ka_used", 1)
        ch_l, ch_a, ch_s = ev("vector_order_layer", CH_L), ev("vector_order_prompt", CH_A), ev("vector_order_batch", CH_S)
        y_mm, y_add = ev("y_products", 2 * NT), ev("y_added", 2 * NT)
        u_mm, u_relu, u_sq = ev("u_products", 32), ev("u_relu", 32), ev("u_squared", 32)
        d_mm, d_add = ev("down_products", 2 * NT), ev("down_added", 2 * NT)
        d_chunk = ev("down_chunks", 6)
        fin, fin_out = ev("final_rows", NT), [load_sem(f"final_stored{n}", 1) for n in range(2)]
        win_out = load_sem("window_state_stored", 0)
        waits_taken_sp, waits_taken_act, waits_taken_pool, waits_taken_pe, waits_taken_dve = (
            ctx.enter_context(nc.semaphore(f"waits_taken_{e}")) for e in ("sp", "act", "pool", "pe", "dve"))
        by_engine = {
            "sync": [c_ld, x_ld, gain_ld, comp_ld, *w_ld, copies, raw_p, raw_ld, sel_ld, win_ld, kda_ld, kdb_ld, vd_ld, win_out],
            "scalar": [sq, xn_rdy, z_stg, g_exp, hexp_p, a_e, a_pt, s_hexp, s_exp, u_relu, *z_out, *fin_out],
            "gpsimd": [rstd, z_v, relay, s_bm, u_sq, a_q, s_q],
            "tensor": [n_tr, z_mm, z_tr, sg_mm, pb_mm, ct_p, hid_p, kvc_p, a_s, a_t, a_o, og_t, td_full,
                       sc_full, oa_full, od_full, y_mm, u_mm, d_mm, d_chunk, win_pv, kda_used],
            "vector": [cleared, h_rdy, z_te, g_rdy, sg_rdy, pb_rdy, xt_p, hdone_p, kvc_pk, a_sb, a_w, a_acc, a_bias, og_k,
                       td_used, sc_used, s_max, s_mask, s_gs, s_diag, out_put, ch_l, ch_a, ch_s, y_add, d_add, fin],
        }

        def begin(eng, name):
            for c in by_engine[name]:
                eng.sem_inc(c.sem, 1)

        block = ctx.enter_context(nc.Block())

        def z_kind(n):
            return Z_CHUNKS[n // NT][0], n % NT

        def a_step(s):
            return s // 12, s % 12 // 4, s % 4

        @block.sync
        def _(sp):
            begin(sp, "sync")

            for n, t in const.items():
                sp.dma_start(t[:], i[n]).then_inc(c_ld.sem, 16)
            sp.dma_start(pages[0:1, :], i["page_table"].rearrange("(o b) g -> o (b g)", o=1)).then_inc(c_ld.sem, 16)
            sp.dma_start(x[:, 0:4, :], i["x_prompt"][0].rearrange("(t p) d -> p t d", p=P)).then_inc(x_ld.sem, 16)
            sp.dma_start(x[0:64, 4, :], i["x_sample"].rearrange("b t d -> (b t) d")).then_inc(x_ld.sem, 16)
            sp.wait_ge(c_ld.sem, c_ld.at(0, len(const) + 1))

            def wait_used(l, n):
                if n == -2:
                    sp.wait_ge(d_chunk.sem, d_chunk.at(l, 0))
                elif n == -1:
                    sp.wait_ge(d_mm.sem, d_mm.at(l, 0))
                elif n < W_OUT0:
                    sp.wait_ge(z_mm.sem, z_mm.at(l, NT * (n + 1)))
                elif n < W_UP0:
                    sp.wait_ge(y_mm.sem, y_mm.at(l, NT * (n - W_OUT0 + 1)))
                elif n < W_DN0:
                    sp.wait_ge(u_mm.sem, u_mm.at(l, 4 * (n - W_UP0 + 1)))
                elif (n - W_DN0) % 4 == 3:
                    sp.wait_ge(d_mm.sem, d_mm.at(l, NT * ((n - W_DN0) // 4 + 1)))
                else:
                    sp.wait_ge(d_chunk.sem, d_chunk.at(l, (n - W_DN0) // 4 * 3 + (n - W_DN0) % 4 + 1))

            with sp.Fori(0, DEPTH) as l:
                L = ds(l, 1)

                def chunk(n, src):
                    wait_used(l, n - 2)
                    width = src.shape[-1]
                    dst = ring[:, n % 2, :].rearrange("p (k c) -> p k c", k=KT)[:, :, 0:width]
                    sp.dma_start(dst, src).then_inc(w_ld[n % 2].sem, 16)
                    copy_state(n)

                def copy_state(n):
                    b, r = n // 3, n % 3
                    rows = (PAST - NS) // 3
                    sp.dma_start(
                        o["dil_s"][L, b, r * rows:(r + 1) * rows].rearrange("o r f -> (o r) f"),
                        i["state_kv_dil"][L, b, NS + r * rows:NS + (r + 1) * rows].rearrange("o r f -> (o r) f")).then_inc(
                            copies.sem, 16)

                wait_used(l, -1)
                sp.dma_start(gain[:, 0, :], i["norm_attn"][L].rearrange("o p k -> (o p) k")).then_inc(gain_ld.sem, 16)
                sp.dma_start(gain[:, 1, :], i["norm_mlp"][L].rearrange("o p k -> (o p) k")).then_inc(gain_ld.sem, 16)
                for n, (_, a, z) in enumerate(Z_CHUNKS):
                    chunk(n, i["w_in"][L, :, a:z].rearrange("o (k p) c -> p (o k) c", p=P))
                    if n == 0:
                        sp.dma_start(pe_in[:].rearrange("p s i -> p (s i)"),
                                     i["cmp_pe"][L].rearrange("o p f -> (o p) f")).then_inc(comp_ld.sem, 16)
                        sp.dma_start(w1[:].rearrange("p s i h -> p (s i h)"),
                                     i["cmp_w1"][L].rearrange("o p f -> (o p) f")).then_inc(comp_ld.sem, 16)
                        sp.dma_start(w2[:].rearrange("p s d -> p (s d)"),
                                     i["cmp_w2"][L].rearrange("o p f -> (o p) f")).then_inc(comp_ld.sem, 16)
                        for b in range(NB):
                            sp.dma_start(
                                o["win_s"][L, b, 0:WIN - NS].rearrange("o r f -> (o r) f"),
                                i["state_kv_win"][L, b, NS:WIN].rearrange("o r f -> (o r) f")).then_inc(
                                    win_out.sem, 16)

                for t in range(4):
                    n = NT + t
                    sp.wait_ge(z_out[n % STG].sem, z_out[n % STG].at(l, store_at[n]))
                    sp.sem_inc(waits_taken_sp, 1)
                wait_used(l, W_OUT0 - 1)
                sp.dma_start(raw[0:NCK_P, :], o["cmp_p"][L, 0].rearrange("o (n c) f -> (o n) (c f)", c=16)).then_inc(
                    raw_p.sem, 16)

                def page_rows(b, cache, dst, sem):
                    for g in range(NPG):
                        page = sp.value_load(pages[0:1, ds(b * NPG + g, 1)], min_val=0, max_val=POOL - 1)
                        sp.dma_start(dst[:, g, :], i[cache][L, ds(page, 1)].rearrange("o q p f -> (o q p) f")).then_inc(
                            sem.sem, 16)

                def of_batch(name, b):
                    return i[name][L, ds(b, 1)].rearrange("o q p g f -> (o q p) g f")

                def load_raw(b):
                    page_rows(b, "cache_kv_cmp", raw.rearrange("p (g f) -> p g f", g=NPG), raw_ld)

                def load_selected(b):
                    page_rows(b, "cache_kv_sel", kvsel, sel_ld)

                def load_window(b):
                    sp.dma_start(kw_sb, of_batch("window_tiles", b)).then_inc(win_ld.sem, 16)

                def load_dilated_k(b):
                    sp.dma_start(kda, of_batch("dilated_k", b)[:, 0:ND_A, :]).then_inc(kda_ld.sem, 16)
                    sp.dma_start(kdb, of_batch("dilated_k", b)[:, ND_A:ND_A + 4, :]).then_inc(kdb_ld.sem, 16)

                def load_dilated_k_rest(b):
                    sp.wait_ge(kda_used.sem, kda_used.at(l * NB + b, 1))
                    sp.dma_start(kda[:, 0:4, :], of_batch("dilated_k", b)[:, ND_A + 4:, :]).then_inc(kda_ld.sem, 16)

                def load_dilated_v(b):
                    sp.dma_start(vd, of_batch("dilated_v", b)).then_inc(vd_ld.sem, 16)

                load_selected(0)
                sp.wait_ge(relay.sem, relay.at(l, 2))
                sp.sem_inc(waits_taken_sp, 1)
                load_raw(0)
                for s in range(STG):
                    sp.wait_ge(z_out[s].sem, z_out[s].at(l, slot_n[s]))
                    sp.sem_inc(waits_taken_sp, 1)
                sp.wait_ge(z_v.sem, z_v.at(l, 3 * NT))
                sp.wait_ge(z_tr.sem, z_tr.at(l, NZT))
                load_window(0)
                sp.wait_ge(og_k.sem, og_k.at(l, 8))
                load_dilated_k(0)
                load_dilated_v(0)
                with sp.Fori(0, NB - 1) as b:
                    it = l * NB + b
                    sp.wait_ge(sc_full.sem, sc_full.at(it, SC_HID + 2))
                    load_raw(b + 1)
                    load_dilated_k_rest(b)
                    sp.wait_ge(sc_full.sem, sc_full.at(it, SC_ST + 1))
                    load_dilated_k(b + 1)
                    sp.wait_ge(win_pv.sem, win_pv.at(it, 1))
                    sp.wait_ge(od_full.sem, od_full.at(it, 1))
                    load_window(b + 1)
                    load_dilated_v(b + 1)
                    sp.wait_ge(oa_full.sem, oa_full.at(it, 1))
                    sp.sem_inc(waits_taken_sp, 1)
                    load_selected(b + 1)
                load_dilated_k_rest(NB - 1)

                for half in range(2):
                    n = W_OUT0 + half
                    if half == 0:
                        sp.wait_ge(sc_full.sem, sc_full.at(l * NB + NB - 1, SC_HID + 2))
                        sp.sem_inc(waits_taken_sp, 1)
                    else:
                        sp.wait_ge(oa_full.sem, oa_full.at(l * NB + NB - 1, 1))
                    chunk(n, i["w_out"][L, :, half * CH:(half + 1) * CH].rearrange("o (k p) c -> p (o k) c", p=P))
                for n in range(W_UP0, W_DN0):
                    c = n - W_UP0
                    chunk(n, i["w_up"][L, :, c * CH:(c + 1) * CH].rearrange("o (k p) c -> p (o k) c", p=P))
                for n in range(W_DN0, W_ALL):
                    half, c = (n - W_DN0) // 4, (n - W_DN0) % 4
                    chunk(n, i["w_down"][L, c * D:(c + 1) * D, half * CH:(half + 1) * CH].rearrange(
                        "o (k p) c -> p (o k) c", p=P))
            sp.wait_ge(d_mm.sem, d_mm.at(DEPTH - 1, 2 * NT))
            sp.dma_start(gfin, i["norm_final"].rearrange("(o d) -> o d", o=1).broadcast_to([P, D])).then_inc(
                c_ld.sem, 16)
            sp.wait_ge(copies.sem, copies.at(0, DEPTH * W_ALL))
            sp.wait_ge(win_out.sem, win_out.at(0, DEPTH * NB))

        @block.scalar
        def _(act):
            begin(act, "scalar")
            copy = nc.scalar.copy
            act.wait_ge(c_ld.sem, c_ld.at(0, len(const) + 1))
            act.wait_ge(x_ld.sem, x_ld.at(0, 2))
            act.wait_ge(cleared.sem, cleared.at(0, 1))

            def values_before(n):
                return sum(z_kind(q)[0] in ("cs", "wg", "vb") for q in range(n))

            def norm_rows(r):
                for t in range(NT):
                    R = ROWS[t]
                    nc.scalar.activation(xn[0:R, t % 2, :], x[0:R, t, :], ACT.Square,
                                         accum_out=stat[0:R, t:t + 1]).then_inc(sq.sem, 1)
                    act.wait_ge(sq.sem, sq.at(r, t + 1))
                act.wait_ge(rstd.sem, rstd.at(r, 2))
                for t in range(NT):
                    R = ROWS[t]
                    if t >= 2:
                        act.wait_ge(n_tr.sem, n_tr.at(r, 2 * (t - 1)))
                    nc.scalar.mul(xn[0:R, t % 2, :], x[0:R, t, :], stat[0:R, 8 + t:9 + t]).then_inc(xn_rdy.sem, 1)

            def out_rows(n, l):
                kind, t = z_kind(n)
                R, L = ROWS[t], ds(l, 1)
                s = stg[:, n % STG, :]

                def put(name, cols, lo=0, hi=None):
                    if t < 4:
                        dst = o[name + "_p"][L, 0, t * P:(t + 1) * P, lo:hi].rearrange("o r f -> (o r) f")
                    elif name in ("win", "dil"):
                        keep = (WIN if name == "win" else PAST) - NS
                        dst = o[name + "_s"][L, :, keep:keep + NS, lo:hi].rearrange("o b r f -> (o b) r f")
                    else:
                        dst = o[name + "_s"][L, :, :, lo:hi].rearrange("o b r f -> (o b) r f")
                    act.dma_start(dst, s[0:R, cols[0]:cols[1]]).then_inc(z_out[n % STG].sem, 16)
                if kind == "cs":
                    put("cmp", (0, 256), 0, 256)
                    put("sel", (256, 512), 0, 256)
                if kind == "wg":
                    put("win", (0, 256), 0, 256)
                if kind == "kb":
                    put("dil", (0, 512), 0, 512)
                if kind == "vb":
                    put("dil", (0, 512), 512, 1024)

            def project(l):
                for n in range(NZ):
                    kind, t = z_kind(n)
                    R = ROWS[t]
                    width = Z_CHUNKS[n // NT][2] - Z_CHUNKS[n // NT][1]
                    s, z = stg[0:R, n % STG, 0:width], bank[4 + n % 2][0:R, 0:width]
                    if n >= STG:
                        act.wait_ge(z_tr.sem, z_tr.at(l, min(n - STG + 1, NZT)))
                        act.wait_ge(z_v.sem, z_v.at(l, values_before(n - STG + 1)))
                        act.wait_ge(z_out[n % STG].sem, z_out[n % STG].at(l, store_at[n - STG]))
                    act.wait_ge(z_mm.sem, z_mm.at(l, n + 1))
                    if kind == "qa":
                        nc.scalar.activation(
                            s.rearrange("p (g k d) -> p k g d", g=4, k=2),
                            z.rearrange("p (k g d) -> p k g d", g=4, k=2), ACT.Copy, scale=SCALE).then_inc(
                                z_stg.sem, 1)
                    elif kind == "qb":
                        nc.scalar.activation(s, z, ACT.Copy, scale=SCALE).then_inc(z_stg.sem, 1)
                    else:
                        if kind == "wg":
                            nc.scalar.activation(gate[0:R, t, :], z[:, 256:280], ACT.Exp, scale=-1.0).then_inc(
                                g_exp.sem, 1)
                        copy(s, z).then_inc(z_stg.sem, 1)
                        act.wait_ge(z_stg.sem, z_stg.at(l, n + 1))
                        out_rows(n, l)

            def prompt_steps(l, base, count):
                for m in range(count + 1):
                    if m < count:
                        w = step_keys(count, m)
                        act.wait_ge(a_sb.sem, a_sb.at(l, base + m + 1))
                        nc.scalar.activation(
                            p_sb[:, m % 4, 0:w], p_sb[:, m % 4, 0:w], ACT.Exp, scale=-1.0,
                            bias=stat[:, 16 + m % 4:17 + m % 4], accum_out=stat[:, 20 + m % 4:21 + m % 4]).then_inc(
                                a_e.sem, 1)
                    if m >= 1:
                        k = m - 1
                        w = step_keys(count, k)
                        act.wait_ge(a_t.sem, a_t.at(l, base + k + 1))
                        act.wait_ge(a_o.sem, a_o.at(l, base + max(k - 1, 0)))
                        cmp = w == NCK_P
                        R, cols = (NCK_P, P) if cmp else (P, w)
                        copy(p_pt[0:R, k % 2, 0:cols], bank[2 + k % 2][0:R, 0:cols]).then_inc(a_pt.sem, 1)

            with act.Fori(0, DEPTH) as l:
                norm_rows(l * 2)
                project(l)
                for s in range(2):
                    act.wait_ge(pb_rdy.sem, pb_rdy.at(l, 2))
                    act.wait_ge(hid_p.sem, hid_p.at(l, s + 1))
                    act.wait_ge(hdone_p.sem, hdone_p.at(l, s))
                    nc.scalar.activation(he[:, 0:2 * NCK_P], bank[2 + s][:, 0:2 * NCK_P], ACT.Exp,
                                         scale=-1.0, bias=ncbias[:, s:s + 1]).then_inc(hexp_p.sem, 1)
                with act.Fori(0, 4) as g:
                    prompt_steps(l, g * STEPS_A, STEPS_A)
                with act.Fori(0, 4) as g:
                    prompt_steps(l, g * STEPS_D + 4 * STEPS_A, STEPS_D)

                with act.Fori(0, NB) as b:
                    it = l * NB + b
                    for s in range(2):
                        act.wait_ge(sc_full.sem, sc_full.at(it, SC_HID + s + 1))
                        act.wait_ge(sc_used.sem, sc_used.at(it, SC_HID + s))
                        nc.scalar.activation(
                            he.rearrange("p (k n) -> p k n", k=2),
                            bank[2 + s][:, 0:258].rearrange("p (k n) -> p k n", k=2)[:, :, 1:129],
                            ACT.Exp, scale=-1.0, bias=ncbias[:, s:s + 1]).then_inc(s_hexp.sem, 1)

                    def probs(scores, n):
                        nc.scalar.activation(scores, scores, ACT.Exp, scale=-1.0, bias=stat[0:64, 23 + n:24 + n],
                                             accum_out=stat[0:64, 27 + n:28 + n]).then_inc(s_exp.sem, 1)
                    act.wait_ge(sc_used.sem, sc_used.at(it, SC_S + 1))
                    probs(s_c, EX_CMP)
                    act.wait_ge(s_max.sem, s_max.at(it, 1))
                    probs(s_win, EX_WIN)
                    act.wait_ge(td_used.sem, td_used.at(it, TD_SD + 1))
                    probs(s_d, EX_DIL)
                    act.wait_ge(s_max.sem, s_max.at(it, 2))
                    probs(s_sel, EX_SEL)

                act.wait_ge(y_add.sem, y_add.at(l, 2 * NT))
                norm_rows(l * 2 + 1)
                with act.Fori(0, 8) as c:
                    for q in range(4):
                        f = c * 4 + q
                        act.wait_ge(u_mm.sem, u_mm.at(l, f + 1))
                        v = uT[:, ds(f, 1), :].rearrange("p o t -> p (o t)")
                        nc.scalar.activation(v[:, 0:SEQ], bank[2 * (q % 2)][:], ACT.Relu)
                        nc.scalar.activation(v[:, SEQ:TOK], bank[2 * (q % 2) + 1][:, 0:ROWS_S], ACT.Relu).then_inc(
                            u_relu.sem, 1)
                act.wait_ge(d_add.sem, d_add.at(l, 2 * NT))
            r = 2 * DEPTH
            for t in range(NT):
                R = ROWS[t]
                nc.scalar.activation(xn[0:R, t % 2, :], x[0:R, t, :], ACT.Square,
                                     accum_out=stat[0:R, t:t + 1]).then_inc(sq.sem, 1)
                act.wait_ge(sq.sem, sq.at(r, t + 1))
            for t in range(NT):
                R = ROWS[t]
                act.wait_ge(fin.sem, fin.at(0, t + 1))
                dst = o["y_p"][0, t * P:(t + 1) * P, :] if t < 4 else o["y_s"].rearrange("b t d -> (b t) d")
                act.dma_start(dst, x[0:R, t, :]).then_inc(fin_out[t % 2].sem, 16)
            act.wait_ge(fin_out[0].sem, fin_out[0].at(0, 3))
            act.wait_ge(fin_out[1].sem, fin_out[1].at(0, 2))
            for s in range(STG):
                act.wait_ge(z_out[s].sem, z_out[s].at(DEPTH - 1, slot_n[s]))

        @block.gpsimd
        def _(pool):
            begin(pool, "gpsimd")

            def row_scale(r):
                pool.wait_ge(sq.sem, sq.at(r, NT))
                pool.sem_inc(waits_taken_pool, 1)
                nc.gpsimd.tensor_scalar(stat[:, 8:8 + NT], stat[:, 0:NT], 1.0 / D, EPS, ALU.mult, ALU.add).then_inc(
                    rstd.sem, 1)
                pool.wait_ge(rstd.sem, rstd.at(r, 1))
                nc.gpsimd.tensor_tensor(stat[:, 8:8 + NT], stat[:, 8:8 + NT], const["mhalf"][:], ALU.pow).then_inc(
                    rstd.sem, 1)

            def relayout(rows, s):
                src = raw[0:rows, :].rearrange("p (c s k d) -> p s k c d", c=16, s=2, k=2)[:, s]
                nc.gpsimd.tensor_copy(
                    relaid[0:rows, :].rearrange("p (k c d) -> p k c d", k=2, c=16), src).then_inc(relay.sem, 1)

            pool.wait_ge(c_ld.sem, c_ld.at(0, len(const) + 1))
            with pool.Fori(0, DEPTH) as l:
                row_scale(l * 2)
                for n in range(NZ):
                    kind, t = z_kind(n)
                    if kind not in ("cs", "wg", "vb"):
                        continue
                    R = ROWS[t]
                    src, at, w = {"cs": (384, 0, 128), "wg": (128, 128, 128), "vb": (0, 256, 512)}[kind]
                    dst = vst[:, t, at:at + w] if t < 4 else vsm[:, at:at + w]
                    pool.wait_ge(z_stg.sem, z_stg.at(l, n + 1))
                    pool.sem_inc(waits_taken_pool, 1)
                    nc.gpsimd.tensor_copy(dst, stg[0:R, n % STG, src:src + w]).then_inc(z_v.sem, 1)
                pool.wait_ge(raw_p.sem, raw_p.at(l, 1))
                pool.sem_inc(waits_taken_pool, 1)
                relayout(NCK_P, 0)
                pool.wait_ge(ct_p.sem, ct_p.at(l, 4))
                pool.sem_inc(waits_taken_pool, 1)
                relayout(NCK_P, 1)
                pool.wait_ge(z_te.sem, z_te.at(l, NZT))
                pool.sem_inc(waits_taken_pool, 1)
                for first, qT in ((0, qaT), (4, qbT)):
                    with pool.Fori(0, 4) as g:
                        pool.wait_ge(a_s.sem, a_s.at(l, g * STEPS_A if first == 0 else g * STEPS_D + 4 * STEPS_A))
                        if first:
                            nc.gpsimd.tensor_copy(p_k, kbT[:, ds(g, 1), :].rearrange("p o c -> p (o c)"))
                        nc.gpsimd.tensor_copy(p_q, qT[:, ds(g, 1), :].rearrange("p o c -> p (o c)")).then_inc(
                            a_q.sem, 1)
                with pool.Fori(0, NB) as b:
                    it = l * NB + b
                    pool.wait_ge(sc_full.sem, sc_full.at(it, 0))
                    nc.gpsimd.tensor_copy(q_s[:], qd[:, ds(b, 1), :].rearrange("p o r -> p (o r)")).then_inc(
                        s_q.sem, 1)
                    pool.wait_ge(s_mask.sem, s_mask.at(it, 1))
                    nc.gpsimd.tensor_tensor(
                        biasm.rearrange("p (j c) -> p j c", j=32), const["b_sel"][:].rearrange("p (j c) -> p j c", j=32),
                        stat[0:64, 32:64].unsqueeze(2).to_broadcast([64, 32, 64]), ALU.add).then_inc(s_bm.sem, 1)
                row_scale(l * 2 + 1)
                with pool.Fori(0, 8) as c:
                    for q in range(4):
                        f = c * 4 + q
                        v = uT[:, ds(f, 1), :].rearrange("p o t -> p (o t)")
                        pool.wait_ge(u_relu.sem, u_relu.at(l, f + 1))
                        nc.gpsimd.tensor_tensor(v, v, v, ALU.mult).then_inc(u_sq.sem, 1)
            row_scale(2 * DEPTH)

        @block.tensor
        def _(pe):
            begin(pe, "tensor")
            mm, tr = nc.tensor.matmul, nc.tensor.transpose

            def norm_transposes(r):
                for t in range(NT):
                    R = ROWS[t]
                    pe.wait_ge(xn_rdy.sem, xn_rdy.at(r, t + 1))
                    for half in range(2):
                        if t >= 2:
                            pe.wait_ge(h_rdy.sem, h_rdy.at(r, 2 * (t - 2) + half + 1))
                            pe.sem_inc(waits_taken_pe, 1)
                        B = bank[2 * (t % 2) + half]
                        for j in range(4):
                            k = half * 4 + j
                            last = tr(B[:, j * P:j * P + R], xn[0:R, t % 2, k * P:(k + 1) * P], ident[0:R, 0:R])
                        last.then_inc(n_tr.sem, 1)

            def rows_times_chunk(dst, t, n, width, start=True, stop=True):
                for k in range(KT):
                    last = mm(dst, hT[:, k, t * P:t * P + ROWS[t]], ring[:, n % 2, k * CH:k * CH + width],
                              start=start and k == 0, stop=stop and k == KT - 1)
                return last

            def z_transposes(l, n):
                kind, t = z_kind(n)
                if kind == "vb":
                    return
                R = ROWS[t]
                s, B = stg[0:R, n % STG, :], bank[6 + n % 2]
                pe.wait_ge(z_stg.sem, z_stg.at(l, n + 1))
                if n >= 2:
                    pe.wait_ge(z_te.sem, z_te.at(l, n - 1))
                    pe.sem_inc(waits_taken_pe, 1)
                first = {"cs": 256}.get(kind, 0)
                for j in range({"cs": 1, "wg": 1}.get(kind, 4)):
                    last = tr(B[:, j * P:j * P + R], s[:, first + j * P:first + (j + 1) * P], ident[0:R, 0:R])
                last.then_inc(z_tr.sem, 1)

            def project(l):
                pe.wait_ge(h_rdy.sem, h_rdy.at(l * 2, 2 * NT))
                for n in range(NZ + 1):
                    if n < NZ:
                        c, t = n // NT, n % NT
                        width = Z_CHUNKS[c][2] - Z_CHUNKS[c][1]
                        if t == 0:
                            w_arrived(l, c)
                        if n >= 2:
                            pe.wait_ge(z_stg.sem, z_stg.at(l, n - 1))
                        last = rows_times_chunk(bank[4 + n % 2][0:ROWS[t], 0:width], t, c, width)
                        last.then_inc(z_mm.sem, 1)
                    if n >= 1:
                        z_transposes(l, n - 1)

            def w_arrived(l, n):
                pe.wait_ge(w_ld[n % 2].sem, w_ld[n % 2].at(l, n // 2 + 1))

            def compress_bias(l):
                pe.wait_ge(comp_ld.sem, comp_ld.at(l, 3))
                pe.wait_ge(z_te.sem, z_te.at(l, NZT))
                for s in range(2):
                    for j in range(16):
                        last = mm(bank[6][:, s:s + 1], w1[:, s, j, :], pe_in[:, s, j:j + 1],
                                  start=(s == 0 and j == 0), stop=(s == 1 and j == 15), skip_group_check=True)
                last.then_inc(pb_mm.sem, 1)

            def compress(n, s, B, full, used, rnd, base, hid_bank, hid_ev):
                for j in range(4):
                    u = base + j
                    pe.wait_ge(used.sem, used.at(rnd, max(u - 1, 0)))
                    pe.sem_inc(waits_taken_pe, 1)
                    for q in range(4):
                        k, pair = j // 2, (j % 2) * 4 + q
                        last = tr(B[u % 2][:, q * n:(q + 1) * n],
                                  relaid[0:n, (k * 8 + pair) * P:(k * 8 + pair + 1) * P], ident[0:n, 0:n])
                    last.then_inc(full.sem, 1)
                pe.wait_ge(used.sem, used.at(rnd, base + 4))
                xt = part(xt_at, 2, 8, n)
                out = hid_bank[:, 0:2 * n].rearrange("p (k n) -> p k n", k=2)
                for j in range(8):
                    mm(out, w1[:, s, j, :], xt[:, :, j, :], start=(j == 0), stop=False, skip_group_check=True)
                for j in range(8):
                    last = mm(out[:, :, 0:n - 1], w1[:, s, 8 + j, :], xt[:, :, j, 1:n], start=False, stop=(j == 7),
                              skip_group_check=True)
                last.then_inc(hid_ev.sem, 1)

            def prompt_steps(l, base, count, kT_of, v_of, pair):
                pe.wait_ge(a_q.sem, a_q.at(l, pair + 1))
                for m in range(count + 2):
                    if m < count:
                        half, w = (m // 12 if count == STEPS_A else m // 4), step_keys(count, m)
                        t = m % 4
                        pe.wait_ge(a_sb.sem, a_sb.at(l, base + max(m - 1, 0)))
                        rows = slice(64 * half, 64 * half + 64)
                        mm(bank[m % 2][:, 0:w], p_q[rows, t * P:(t + 1) * P], kT_of(m, rows, w),
                            start=True, stop=True).then_inc(a_s.sem, 1)
                    if 1 <= m <= count:
                        k = m - 1
                        w = step_keys(count, k)
                        pe.wait_ge(a_e.sem, a_e.at(l, base + k + 1))
                        pe.wait_ge(a_pt.sem, a_pt.at(l, base + max(k - 1, 0)))
                        if w == NCK_P:
                            last = tr(bank[2 + k % 2][0:w, 0:P], p_sb[:, k % 4, 0:w], ident[:])
                        else:
                            for c in range(w // P):
                                last = tr(bank[2 + k % 2][:, c * P:(c + 1) * P], p_sb[:, k % 4, c * P:(c + 1) * P], ident[:])
                        last.then_inc(a_t.sem, 1)
                    if m >= 2:
                        k = m - 2
                        w = step_keys(count, k)
                        pe.wait_ge(a_pt.sem, a_pt.at(l, base + k + 1))
                        pe.wait_ge(a_acc.sem, a_acc.at(l, base + max(k - 1, 0)))
                        dst = bank[4 + k % 2][:, 0:HD]
                        if w == NCK_P:
                            last = mm(dst, p_pt[0:w, k % 2, 0:P], v_of(k, 0), start=True, stop=True)
                        else:
                            for c in range(w // P):
                                last = mm(dst, p_pt[:, k % 2, c * P:(c + 1) * P], v_of(k, c),
                                          start=(c == 0), stop=(c == w // P - 1))
                        last.then_inc(a_o.sem, 1)

            def pair_transposes(l, g, base, count):
                pe.wait_ge(a_acc.sem, a_acc.at(l, base + count))
                pe.wait_ge(og_k.sem, og_k.at(l, g))
                for t in range(4):
                    last = tr(bank[6][:, t * P:(t + 1) * P], og[:, t, :], ident[:])
                last.then_inc(og_t.sem, 1)

            pe.wait_ge(c_ld.sem, c_ld.at(0, len(const) + 1))
            with pe.Fori(0, DEPTH) as l:
                norm_transposes(l * 2)
                project(l)
                compress_bias(l)
                for s in range(2):
                    pe.wait_ge(relay.sem, relay.at(l, s + 1))
                    compress(NCK_P, s, [bank[0], bank[1]], ct_p, xt_p, l, 4 * s, bank[2 + s], hid_p)
                pe.wait_ge(hdone_p.sem, hdone_p.at(l, 1))
                for k in range(2):
                    last = mm(bank[4][64 * k:64 * k + 64, 0:NCK_P], w2[:, 0, :], hid[:, 0, k * NCK_P:(k + 1) * NCK_P],
                              start=True, stop=True)
                last.then_inc(kvc_p.sem, 1)
                pe.wait_ge(hdone_p.sem, hdone_p.at(l, 2))
                for k in range(2):
                    last = mm(bank[5][0:NCK_P, k * HD:(k + 1) * HD], hid[:, 1, k * NCK_P:(k + 1) * NCK_P], w2[:, 1, :],
                              start=True, stop=True)
                last.then_inc(kvc_p.sem, 1)
                pe.wait_ge(sg_rdy.sem, sg_rdy.at(l, 1))
                pe.sem_inc(waits_taken_pe, 1)
                mm(bank[6][0:64, 0:192], const["tsel"][:], gb, start=True, stop=True).then_inc(sg_mm.sem, 1)
                pe.wait_ge(kvc_pk.sem, kvc_pk.at(l, 2))
                pe.wait_ge(z_te.sem, z_te.at(l, NZT))
                pe.wait_ge(z_v.sem, z_v.at(l, 3 * NT))
                pe.wait_ge(sg_rdy.sem, sg_rdy.at(l, 2))
                pe.sem_inc(waits_taken_pe, 1)
                with pe.Fori(0, 4) as g:
                    def keys_a(m, rows, w):
                        br = a_step(m)[1]
                        return ktcp[rows, :] if br == 0 else (ksT if br == 1 else kwT)[rows, 0:w]

                    def values_a(m, c):
                        k, br, _ = a_step(m)
                        return (vcp[:, k * HD:(k + 1) * HD] if br == 0 else
                                vst[:, c, (br - 1) * 128 + k * HD:(br - 1) * 128 + (k + 1) * HD])
                    prompt_steps(l, g * STEPS_A, STEPS_A, keys_a, values_a, g)
                    pair_transposes(l, g, g * STEPS_A, STEPS_A)
                with pe.Fori(0, 4) as g:
                    def keys_d(m, rows, w):
                        return p_k[rows, 0:w]

                    def values_d(m, c):
                        return vst[:, c, ds(256 + (m // 4) * HD + g * 128, HD)]
                    prompt_steps(l, g * STEPS_D + 4 * STEPS_A, STEPS_D, keys_d, values_d, g + 4)
                    pair_transposes(l, g + 4, g * STEPS_D + 4 * STEPS_A, STEPS_D)

                with pe.Fori(0, NB) as b:
                    it = l * NB + b



                    pe.wait_ge(raw_ld.sem, raw_ld.at(it, NPG))
                    for s in range(2):
                        pe.wait_ge(sc_used.sem, sc_used.at(it, max(SC_HID + s - 3, 0)))
                        out = bank[2 + (SC_HID + s) % 4][:, 0:258].rearrange("p (k n) -> p k n", k=2)
                        for j in range(16):
                            first = 1 if j < 8 else 0
                            for k in range(2):
                                last = mm(out[:, k, first:first + P], w1[:, s, j, :], rawt[:, :, s, k, j % 8, :],
                                          start=(j == 0 and k == 0), stop=(j == 15 and k == 1), skip_group_check=True)
                        last.then_inc(sc_full.sem, 1)

                    pe.wait_ge(sc_used.sem, sc_used.at(it, max(SC_ST - 3, 0)))
                    S = bank[2 + SC_ST % 4][:, 0:256].rearrange("p (e t h) -> p e t h", e=4, t=8)

                    def qs(p, t0, n, step):
                        v = qdb[:, p, ds(b, 1), :, :].rearrange("p o t h -> p (o t) h")
                        return v[:, t0:t0 + (n - 1) * step + 1:step, :]

                    def queries_of(j):
                        return (0, 0, 8, 1) if j == 0 else (1, j - 1, 2, 4) if j < 5 else (2, j - 5, 1, 1)

                    pe.wait_ge(kda_ld.sem, kda_ld.at(it, 1))
                    for j in range(ND_TILES):
                        if j == ND_A:
                            pe.wait_ge(kdb_ld.sem, kdb_ld.at(it, 1))
                        if j == ND_A + 4:
                            pe.wait_ge(kda_ld.sem, kda_ld.at(it, 2))
                        tile = kdb[:, j - ND_A, :] if ND_A <= j < ND_A + 4 else kda[:, j % (ND_A + 4), :]
                        e, t0, n, step = queries_of(j)
                        for p in range(4):
                            last = mm(S[:, e, t0:t0 + (n - 1) * step + 1:step, 2 * p:2 * p + 2], tile[:, p * P:(p + 1) * P],
                                      qs(p, t0, n, step), start=(j == 0 and p == 0), stop=False, skip_group_check=True)
                        if j == ND_A - 1:
                            last.then_inc(kda_used.sem, 1)
                    for p in range(4):
                        last = mm(S[0:64, 3, :, 2 * p:2 * p + 2], knb[:, p, :], qs(p, 0, 8, 1), start=False,
                                  stop=(p == 3), skip_group_check=True)
                    last.then_inc(sc_full.sem, 1)

                    pe.wait_ge(sc_used.sem, sc_used.at(it, max(SC_KTC - 3, 0)))
                    B = bank[2 + SC_KTC % 4]
                    pe.wait_ge(sc_used.sem, sc_used.at(it, SC_HID + 2))
                    for k in range(2):
                        last = mm(B[64 * k:64 * k + 64, 0:P], w2[:, 0, :], hid[:, 0, k * P:(k + 1) * P], start=True, stop=True)
                    last.then_inc(sc_full.sem, 1)
                    pe.wait_ge(sc_used.sem, sc_used.at(it, max(SC_VC - 3, 0)))
                    B = bank[2 + SC_VC % 4]
                    for k in range(2):
                        last = mm(B[:, k * HD:(k + 1) * HD], hid[:, 1, k * P:(k + 1) * P], w2[:, 1, :],
                                  start=(k == 0), stop=(k == 1), skip_group_check=True)
                    last.then_inc(sc_full.sem, 1)
                    q_a = q_s[:]
                    pe.wait_ge(s_q.sem, s_q.at(it, 1))
                    pe.wait_ge(sc_used.sem, sc_used.at(it, max(SC_S - 3, 0)))
                    B = bank[2 + SC_S % 4]
                    pe.wait_ge(sc_used.sem, sc_used.at(it, SC_KTC + 1))
                    mm(B[0:64, 0:P], q_a, ktc, start=True, stop=True).then_inc(sc_full.sem, 1)
                    pe.wait_ge(win_ld.sem, win_ld.at(it, 1))
                    pe.wait_ge(sc_used.sem, sc_used.at(it, max(SC_WIN - 3, 0)))
                    mm(bank[2 + SC_WIN % 4][0:64, :], q_a, kw_sb[:, :, 0:128], start=True, stop=True).then_inc(
                        sc_full.sem, 1)
                    pe.wait_ge(sc_used.sem, sc_used.at(it, max(SC_WIN + 1 - 3, 0)))
                    mm(bank[2 + (SC_WIN + 1) % 4][0:64, 0:64], q_a, knw[:], start=True, stop=True).then_inc(
                        sc_full.sem, 1)
                    pe.wait_ge(td_used.sem, td_used.at(it, max(TD_SD - 1, 0)))
                    pe.sem_inc(waits_taken_pe, 1)
                    B = bank[TD_SD % 2]
                    pe.wait_ge(sc_used.sem, sc_used.at(it, SC_ST + 1))
                    pe.sem_inc(waits_taken_pe, 1)
                    for e in range(4):
                        R = 64 if e == 3 else P
                        last = tr(B[0:64, e * P:e * P + R], st_sb[0:R, e * 64:(e + 1) * 64], ident[0:R, 0:R])
                    last.then_inc(td_full.sem, 1)
                    pe.wait_ge(sc_used.sem, sc_used.at(it, max(SC_IMP - 3, 0)))
                    pe.sem_inc(waits_taken_pe, 1)
                    B = bank[2 + SC_IMP % 4]
                    pe.wait_ge(s_gs.sem, s_gs.at(it, 1))
                    pe.sem_inc(waits_taken_pe, 1)
                    mm(B[0:64, 0:P], gs[:], s_c, start=True, stop=True).then_inc(sc_full.sem, 1)
                    pe.wait_ge(td_used.sem, td_used.at(it, max(TD_PTC - 1, 0)))
                    pe.sem_inc(waits_taken_pe, 1)
                    tr(bank[TD_PTC % 2][:, 0:64], s_c, ident[0:64, 0:64]).then_inc(td_full.sem, 1)
                    pe.wait_ge(s_exp.sem, s_exp.at(it, EX_WIN))
                    pe.wait_ge(td_used.sem, td_used.at(it, max(TD_PTW - 1, 0)))
                    pe.sem_inc(waits_taken_pe, 1)
                    B = bank[TD_PTW % 2]
                    for c in range(5):
                        R = P if c < 4 else 64
                        last = tr(B[0:R, c * 64:(c + 1) * 64], s_win[:, c * P:c * P + R], ident[0:64, 0:64])
                    last.then_inc(td_full.sem, 1)
                    pe.wait_ge(sel_ld.sem, sel_ld.at(it, NPG))
                    for u in range(4):
                        pe.wait_ge(sc_used.sem, sc_used.at(it, max(SC_SEL + u - 3, 0)))
                        mm(bank[2 + (SC_SEL + u) % 4][0:64, :], q_a, kvsel[:, u * 4:u * 4 + 4, 0:128], start=True, stop=True).then_inc(
                            sc_full.sem, 1)
                    pe.wait_ge(sc_used.sem, sc_used.at(it, max(SC_SEL + 4 - 3, 0)))
                    mm(bank[2 + (SC_SEL + 4) % 4][0:64, 0:64], q_a, kns[:], start=True, stop=True).then_inc(
                        sc_full.sem, 1)
                    pe.wait_ge(s_exp.sem, s_exp.at(it, EX_DIL))
                    pe.wait_ge(td_used.sem, td_used.at(it, max(TD_PTD - 1, 0)))
                    pe.sem_inc(waits_taken_pe, 1)
                    B = bank[TD_PTD % 2]
                    for e in range(4):
                        R = 64 if e == 3 else P
                        last = tr(B[0:R, e * 64:(e + 1) * 64], s_d[:, e * P:e * P + R], ident[0:64, 0:64])
                    last.then_inc(td_full.sem, 1)
                    pe.wait_ge(vd_ld.sem, vd_ld.at(it, 1))
                    pe.wait_ge(out_put.sem, out_put.at(it, 0))
                    pe.wait_ge(td_used.sem, td_used.at(it, TD_PTD + 1))
                    OD = bank[7][:, 0:64].rearrange("p (q t h) -> p q t h", q=4, t=8)
                    for j in range(ND_TILES + 1):
                        e, t0, n, step = queries_of(j) if j < ND_TILES else (3, 0, 8, 1)
                        R = P if j < ND_TILES else 64
                        pv = ptd[0:R, e, :].rearrange("p (t h) -> p t h", t=8)
                        for p in range(4):
                            v = vd[:, j, p * P:(p + 1) * P] if j < ND_TILES else vsm[:, 256 + p * P:256 + (p + 1) * P]
                            sl = slice(t0, t0 + (n - 1) * step + 1, step)
                            last = mm(OD[:, p, sl, :], v, pv[:, sl, 2 * p:2 * p + 2], start=(j == 0 and p == 0),
                                      stop=(j == ND_TILES and p == 3), skip_group_check=True)
                    last.then_inc(od_full.sem, 1)
                    pe.wait_ge(s_diag.sem, s_diag.at(it, 1))
                    pe.wait_ge(sc_used.sem, sc_used.at(it, max(SC_WBD - 3, 0)))
                    mm(bank[2 + SC_WBD % 4][:, 0:64], const["ones"][:], diag[:, 192:256], start=True, stop=True).then_inc(
                        sc_full.sem, 1)
                    O = bank[6][:, 0:192].rearrange("p (e r) -> p e r", e=3)
                    mm(O[:, 0, :], vc, ptc, start=True, stop=False, skip_group_check=True)
                    for c in range(4):
                        mm(O[:, 2, :], kw_sb[:, c, 128:256], ptw[:, c, :], start=False, stop=False, skip_group_check=True)
                    mm(O[:, 2, :], vsm[:, 128:256], ptw[0:64, 4, :], start=False, stop=False,
                        skip_group_check=True).then_inc(win_pv.sem, 1)
                    pe.wait_ge(s_exp.sem, s_exp.at(it, EX_SEL))
                    for u in range(3):
                        pe.wait_ge(td_used.sem, td_used.at(it, max(TD_PTS + u - 1, 0)))
                        pe.sem_inc(waits_taken_pe, 1)
                        B = bank[(TD_PTS + u) % 2]
                        for c in range(u * 8, min(u * 8 + 8, 17)):
                            R = P if c < 16 else 64
                            last = tr(B[0:R, (c % 8) * 64:(c % 8 + 1) * 64], s_sel[:, c * P:c * P + R], ident[0:64, 0:64])
                        last.then_inc(td_full.sem, 1)
                    pe.wait_ge(td_used.sem, td_used.at(it, TD_PTS + 3))
                    for c in range(16):
                        mm(O[:, 1, :], kvsel[:, c, 128:256], pts[:, c, :], start=False, stop=False, skip_group_check=True)
                    mm(O[:, 1, :], vsm[:, 0:128], pts[0:64, 16, :], start=False, stop=True,
                        skip_group_check=True).then_inc(oa_full.sem, 1)
                    pe.wait_ge(s_diag.sem, s_diag.at(it, 2))
                    pe.wait_ge(sc_used.sem, sc_used.at(it, max(SC_WBA - 3, 0)))
                    mm(bank[2 + SC_WBA % 4][:, 0:192], const["ones"][:], diag[:, 0:192], start=True, stop=True).then_inc(
                        sc_full.sem, 1)

                pe.wait_ge(out_put.sem, out_put.at(l * NB + NB - 1, 4))
                for half in range(2):
                    n = W_OUT0 + half
                    w_arrived(l, n)
                    for t in range(NT):
                        if half:
                            pe.wait_ge(y_add.sem, y_add.at(l, t + 1))
                        rows_times_chunk(bank[t][0:ROWS[t], :], t, n, CH).then_inc(y_mm.sem, 1)
                norm_transposes(l * 2 + 1)
                pe.wait_ge(h_rdy.sem, h_rdy.at(l * 2 + 1, 2 * NT))
                pe.sem_inc(waits_taken_pe, 1)
                with pe.Fori(0, 4) as c2:
                    for par in range(2):
                        n = W_UP0 + par
                        pe.wait_ge(w_ld[par].sem, w_ld[par].at(l, c2 + (n // 2 + 1)))
                        for q in range(4):
                            f = c2 * 8 + par * 4 + q
                            A, Bk = bank[2 * (q % 2)], bank[2 * (q % 2) + 1]
                            if q >= 2:
                                pe.wait_ge(u_relu.sem, u_relu.at(l, f - 1))
                            else:
                                pe.wait_ge(u_relu.sem, u_relu.at(l, c2 * 8 + par * 4))
                            for k in range(KT):
                                lhs = ring[:, par, k * CH + q * P:k * CH + (q + 1) * P]
                                mm(A[:], lhs, hT[:, k, 0:SEQ], start=(k == 0), stop=(k == KT - 1))
                                last = mm(Bk[:, 0:ROWS_S], lhs, hT[:, k, SEQ:TOK], start=(k == 0), stop=(k == KT - 1))
                            last.then_inc(u_mm.sem, 1)
                pe.wait_ge(u_sq.sem, u_sq.at(l, 32))
                for n in range(W_DN0, W_ALL):
                    half, c = (n - W_DN0) // 4, (n - W_DN0) % 4
                    w_arrived(l, n)
                    for t in range(NT):
                        if half and c == 0:
                            pe.wait_ge(d_add.sem, d_add.at(l, t + 1))
                        for k in range(8):
                            last = mm(bank[t][0:ROWS[t], :], uT[:, c * 8 + k, t * P:t * P + ROWS[t]],
                                      ring[:, n % 2, k * CH:(k + 1) * CH], start=(c == 0 and k == 0),
                                      stop=(c == 3 and k == 7))
                        if c == 3:
                            last.then_inc(d_mm.sem, 1)
                    if c < 3:
                        last.then_inc(d_chunk.sem, 1)

        @block.vector
        def _(dve):
            begin(dve, "vector")
            V = nc.vector

            class Order:

                def __init__(self, count, rnd, first=0):
                    self.sem, self.count, self.rnd, self.k, self.first = count.sem, count, rnd, 0, first

                def next(self):
                    self.k += 1
                    return self.count.at(self.rnd, self.first + self.k)

            def norm_keep(r, which):
                for t in range(NT):
                    R = ROWS[t]
                    for half in range(2):
                        dve.wait_ge(n_tr.sem, n_tr.at(r, 2 * t + half + 1))
                        V.tensor_tensor(
                            hT[:, half * 4:half * 4 + 4, t * P:t * P + R],
                            bank[2 * (t % 2) + half][:].rearrange("p (j c) -> p j c", j=4)[:, :, 0:R],
                            gain[:, which, half * 4:half * 4 + 4].unsqueeze(2).to_broadcast([P, 4, R]), ALU.mult).then_inc(
                                h_rdy.sem, 1)

            def z_keep(l, n):
                kind, t = z_kind(n)
                dve.wait_ge(z_tr.sem, z_tr.at(l, n + 1))
                B = bank[6 + n % 2]
                cols = slice(t * P, (t + 1) * P)
                by4 = B[:].rearrange("p (g c) -> p g c", g=4)
                if t < 4:
                    if kind in ("cs", "wg"):
                        last = V.tensor_copy((ksT if kind == "cs" else kwT)[:, cols], B[:, 0:P])
                    else:
                        last = V.tensor_copy({"qa": qaT, "qb": qbT, "kb": kbT}[kind][:, :, cols], by4)
                elif kind in ("cs", "wg"):
                    last = V.tensor_copy((kns if kind == "cs" else knw)[:], B[:, 0:64])
                elif kind == "kb":
                    last = V.tensor_copy(knb[:], by4[:, :, 0:64])
                else:
                    for k in range(2):
                        rows = slice(64 * k, 64 * k + 64)
                        if kind == "qa":
                            for g in range(4):
                                last = V.tensor_copy(qd[rows, :, 32 * k + 8 * g:32 * k + 8 * g + 8],
                                                     by4[rows, g, 0:64].rearrange("p (b t) -> p b t", b=NB))
                        else:
                            last = V.tensor_copy(qdb[rows, :, :, :, k].rearrange("p q b t -> p q (b t)"),
                                                 by4[rows, :, 0:64])
                last.then_inc(z_te.sem, 1)

            def hidden(order, n, s, src, done):
                V.tensor_scalar(he[:, 0:2 * n], he[:, 0:2 * n], 1.0, None, ALU.add).then_inc(order.sem, 1)
                dve.wait_ge(order.sem, order.next())
                V.reciprocal(he[:, 0:2 * n], he[:, 0:2 * n]).then_inc(order.sem, 1)
                dve.wait_ge(order.sem, order.next())
                V.scalar_tensor_tensor(hid[:, s, 0:2 * n], src[:, 0:2 * n], cbias[:, s:s + 1],
                                       he[:, 0:2 * n], ALU.add, ALU.mult).then_inc(done.sem, 1)

            def prompt_steps(l, g, base, count, pair, order):
                sparse = count == STEPS_A
                dve.wait_ge(a_sb.sem, a_sb.at(l, base))
                for k in range(2):
                    slope = slopes[:, ds(8 * k + g * 2, 1)] if sparse else slopes[:, ds(g * 4 + (2 * k + 1), 1)]
                    if sparse:
                        V.tensor_scalar(p_biasc[:, k, :], const["ndc"][:], slope, None, ALU.mult)
                        last = V.tensor_scalar(p_bias[:, k, :], const["nd"][:], slope, None, ALU.mult)
                    else:
                        last = V.scalar_tensor_tensor(p_bias[:, k, :], const["nd"][:], slope, const["lnb"][:],
                                                      ALU.mult, ALU.add)
                last.then_inc(a_bias.sem, 1)
                dve.wait_ge(a_bias.sem, a_bias.at(l, pair + 1))
                dve.wait_ge(og_t.sem, og_t.at(l, pair))
                for m in range(count + 2):
                    if m < count:
                        k, t, w = (m // 12 if sparse else m // 4), m % 4, step_keys(count, m)
                        bias = p_biasc[:, k, t * 32:(t + 1) * 32] if w == NCK_P else p_bias[:, k, SEQ - w:SEQ]
                        dve.wait_ge(a_s.sem, a_s.at(l, base + m + 1))
                        dve.wait_ge(a_t.sem, a_t.at(l, base + max(m - 3, 0)))
                        dve.sem_inc(waits_taken_dve, 1)
                        V.tensor_tensor_reduce(p_sb[:, m % 4, 0:w], bank[m % 2][:, 0:w], bias, -1.0, BIG,
                                               ALU.add, ALU.min, stat[:, 16 + m % 4:17 + m % 4]).then_inc(a_sb.sem, 1)
                    if m >= 2:
                        q = m - 2
                        t = q % 4
                        half = q // 12 if sparse else q // 4
                        dve.wait_ge(a_o.sem, a_o.at(l, base + q + 1))
                        rc, w_ = sm[:, q % 4:q % 4 + 1], sm[:, 4 + q % 4:5 + q % 4]
                        V.reciprocal(rc, stat[:, 20 + q % 4:21 + q % 4]).then_inc(order.sem, 1)
                        dve.wait_ge(order.sem, order.next())
                        dst, src = og[:, t, half * HD:(half + 1) * HD], bank[4 + q % 2][:, 0:HD]
                        if sparse:
                            br = a_step(q)[1]
                            gt = gate[:, t, ds(g * 3 + (12 * half + br), 1)]
                            if br == 0 and t == 0:
                                V.scalar_tensor_tensor(w_, rc, const["okrow"][:], gt, ALU.mult, ALU.mult).then_inc(
                                    order.sem, 1)
                                dve.wait_ge(order.sem, order.next())
                            else:
                                V.tensor_tensor(w_, rc, gt, ALU.mult).then_inc(order.sem, 1)
                                dve.wait_ge(order.sem, order.next())
                            if br == 0:
                                last = V.tensor_scalar(dst, src, w_, None, ALU.mult)
                            else:
                                last = V.scalar_tensor_tensor(dst, src, w_, dst, ALU.mult, ALU.add)
                        else:
                            last = V.tensor_scalar(dst, src, rc, None, ALU.mult)
                        last.then_inc(a_acc.sem, 1)
                dve.wait_ge(og_t.sem, og_t.at(l, pair + 1))
                kt = g if sparse else g + 4
                V.tensor_copy(hT[:, ds(kt, 1), 0:SEQ].rearrange("p o c -> p (o c)"), bank[6][:]).then_inc(og_k.sem, 1)

            V.memset(stat[:], 1.0)
            V.memset(topk[:], 0.0)
            V.memset(qd[:], 0.0)
            V.memset(qdb[:], 0.0).then_inc(cleared.sem, 1)
            dve.wait_ge(cleared.sem, cleared.at(0, 1))
            dve.wait_ge(c_ld.sem, c_ld.at(0, len(const) + 1))
            with dve.Fori(0, DEPTH) as l:
                lay = Order(ch_l, l)
                dve.wait_ge(gain_ld.sem, gain_ld.at(l, 2))
                norm_keep(l * 2, 0)
                for n in range(NZT):
                    z_keep(l, n)
                dve.wait_ge(g_exp.sem, g_exp.at(l, NT))
                V.tensor_scalar(gate[:, 0:4, :], gate[:, 0:4, :], 1.0, None, ALU.add)
                V.tensor_scalar(gate[0:64, 4, :], gate[0:64, 4, :], 1.0, None, ALU.add).then_inc(g_rdy.sem, 1)
                dve.wait_ge(g_rdy.sem, g_rdy.at(l, 1))
                V.reciprocal(gate[:, 0:4, :], gate[:, 0:4, :])
                V.reciprocal(gate[0:64, 4, :], gate[0:64, 4, :]).then_inc(g_rdy.sem, 1)
                dve.wait_ge(g_rdy.sem, g_rdy.at(l, 2))
                dve.wait_ge(pb_mm.sem, pb_mm.at(l, 1))
                V.tensor_copy(cbias[:], bank[6][:, 0:2]).then_inc(pb_rdy.sem, 1)
                dve.wait_ge(pb_rdy.sem, pb_rdy.at(l, 1))
                V.tensor_scalar(ncbias[:], cbias[:], -1.0, None, ALU.mult).then_inc(pb_rdy.sem, 1)
                dve.wait_ge(pb_rdy.sem, pb_rdy.at(l, 2))
                for s in range(2):
                    for j in range(4):
                        dve.wait_ge(ct_p.sem, ct_p.at(l, 4 * s + j + 1))
                        if s == 1 and j == 0:
                            dve.wait_ge(hid_p.sem, hid_p.at(l, 1))
                        V.tensor_copy(part(xt_at + j * 4 * NCK_P, 4 * NCK_P), bank[j % 2][:, 0:4 * NCK_P]).then_inc(
                            xt_p.sem, 1)
                    dve.wait_ge(hexp_p.sem, hexp_p.at(l, s + 1))
                    hidden(lay, NCK_P, s, bank[2 + s], hdone_p)
                V.tensor_tensor(
                    gb.rearrange("p (b e) -> p b e", b=NB), const["bsel"][:].unsqueeze(2).to_broadcast([64, NB, 24]),
                    gate[0:64, 4:5, :].to_broadcast([64, NB, 24]), ALU.mult).then_inc(sg_rdy.sem, 1)
                dve.wait_ge(kvc_p.sem, kvc_p.at(l, 1))
                V.tensor_copy(ktcp[:], bank[4][:, 0:NCK_P]).then_inc(kvc_pk.sem, 1)
                dve.wait_ge(kvc_p.sem, kvc_p.at(l, 2))
                V.tensor_copy(vcp[:], bank[5][0:NCK_P, 0:P]).then_inc(kvc_pk.sem, 1)
                dve.wait_ge(sg_mm.sem, sg_mm.at(l, 1))
                V.tensor_tensor(gm, bank[6][0:64, 0:192], const["hsel"][:], ALU.mult).then_inc(sg_rdy.sem, 1)
                dve.wait_ge(sg_rdy.sem, sg_rdy.at(l, 2))
                V.tensor_reduce(sgate[:], gm.rearrange("p (b h e) -> p b e h", b=NB, h=8), X, ALU.add).then_inc(
                    sg_rdy.sem, 1)
                dve.wait_ge(sg_rdy.sem, sg_rdy.at(l, 3))
                dve.sem_inc(waits_taken_dve, 1)

                with dve.Fori(0, 4) as g:
                    prompt_steps(l, g, g * STEPS_A, STEPS_A, g, Order(ch_a, l, g * (2 * STEPS_A)))
                with dve.Fori(0, 4) as g:
                    prompt_steps(l, g, g * STEPS_D + 4 * STEPS_A, STEPS_D, g + 4,
                                 Order(ch_a, l, g * STEPS_D + 8 * STEPS_A))

                with dve.Fori(0, NB) as b:
                    it = l * NB + b
                    order = Order(ch_s, it)
                    new = ds(b * 64, 64)
                    put = ds(b * NS + SEQ, NS)
                    for s in range(2):
                        dve.wait_ge(s_hexp.sem, s_hexp.at(it, s + 1))
                        V.tensor_scalar(he, he, 1.0, None, ALU.add).then_inc(order.sem, 1)
                        dve.wait_ge(order.sem, order.next())
                        V.reciprocal(he, he).then_inc(order.sem, 1)
                        dve.wait_ge(order.sem, order.next())
                        V.scalar_tensor_tensor(
                            hid[:, s, :].rearrange("p (k n) -> p k n", k=2),
                            bank[2 + s][:, 0:258].rearrange("p (k n) -> p k n", k=2)[:, :, 1:129], cbias[:, s:s + 1],
                            he.rearrange("p (k n) -> p k n", k=2), ALU.add, ALU.mult).then_inc(sc_used.sem, 1)



                    def new_scores(dst, src, bias, at):
                        V.scalar_tensor_tensor(dst, src, -1.0, bias, ALU.mult, ALU.add).then_inc(order.sem, 1)
                        dve.wait_ge(order.sem, order.next())
                        return V.tensor_reduce(sm[0:64, at:at + 1], dst, X, ALU.min)

                    def negated(dst, src, bias, least):
                        return V.tensor_tensor_reduce(dst, src, bias, -1.0, BIG, ALU.add, ALU.min, least)

                    dve.wait_ge(sc_full.sem, sc_full.at(it, SC_ST + 1))
                    B = bank[2 + SC_ST % 4]
                    V.tensor_copy(st_sb[:, 0:192], B[:, 0:192])
                    V.tensor_copy(st_sb[0:64, 192:256], B[0:64, 192:256]).then_inc(sc_used.sem, 1)
                    dve.wait_ge(sc_full.sem, sc_full.at(it, SC_KTC + 1))
                    V.tensor_copy(ktc, bank[2 + SC_KTC % 4][:, 0:P]).then_inc(sc_used.sem, 1)
                    dve.wait_ge(sc_full.sem, sc_full.at(it, SC_VC + 1))
                    dve.sem_inc(waits_taken_dve, 1)
                    V.tensor_copy(vc, bank[2 + SC_VC % 4][:, 0:P]).then_inc(sc_used.sem, 1)
                    dve.wait_ge(sc_full.sem, sc_full.at(it, SC_S + 1))
                    dve.sem_inc(waits_taken_dve, 1)
                    negated(s_c, bank[2 + SC_S % 4][0:64, 0:P], const["b_cmp"][:], stat[0:64, 24:25]).then_inc(
                        sc_used.sem, 1)
                    dve.wait_ge(sc_full.sem, sc_full.at(it, SC_WIN + 1))
                    dve.sem_inc(waits_taken_dve, 1)
                    negated(s_win[:, 0:WIN], bank[2 + SC_WIN % 4][0:64, :], const["b_win"][:], sm[0:64, 22:23]).then_inc(
                        sc_used.sem, 1)
                    dve.wait_ge(sc_full.sem, sc_full.at(it, SC_WIN + 1 + 1))
                    new_scores(s_win[:, WIN:WIN + 64], bank[2 + (SC_WIN + 1) % 4][0:64, 0:64],
                               const["nb_newa"][:, new], 23).then_inc(sc_used.sem, 1)
                    dve.wait_ge(sc_used.sem, sc_used.at(it, SC_WIN + 2))
                    V.tensor_reduce(stat[0:64, 25:26], sm[0:64, 22:24], X, ALU.min).then_inc(s_max.sem, 1)
                    dve.wait_ge(td_full.sem, td_full.at(it, TD_SD + 1))
                    dve.sem_inc(waits_taken_dve, 1)
                    B = bank[TD_SD % 2]
                    negated(s_d[:, 0:384], B[0:64, 0:384], const["b_dil"][:], sm[0:64, 24:25])
                    new_scores(s_d[:, 384:448], B[0:64, 384:448], const["nb_newd"][:, new], 25).then_inc(order.sem, 1)
                    dve.wait_ge(order.sem, order.next())
                    V.tensor_reduce(stat[0:64, 26:27], sm[0:64, 24:26], X, ALU.min).then_inc(td_used.sem, 1)
                    dve.wait_ge(s_exp.sem, s_exp.at(it, EX_CMP))
                    V.reciprocal(sm[0:64, 8:9], stat[0:64, 28:29]).then_inc(order.sem, 1)
                    dve.wait_ge(order.sem, order.next())
                    V.tensor_scalar(gs[:], const["gsum"][:], sm[0:64, 8:9], None, ALU.mult).then_inc(s_gs.sem, 1)
                    dve.wait_ge(sc_full.sem, sc_full.at(it, SC_IMP + 1))
                    imp = bank[2 + SC_IMP % 4][0:64, 0:P].rearrange("p (j c) -> p j c", c=4)
                    sc_a, sc_b, sc_c, top = topk[:, 0:33], topk[:, 33:66], topk[:, 66:99], topk[:, 99:107]
                    V.tensor_reduce(sc_a[:, 0:32], imp, X, ALU.add).then_inc(order.sem, 1)
                    dve.wait_ge(order.sem, order.next())
                    V.tensor_tensor(sc_a[:, 1:32], sc_a[:, 1:32], imp[:, 0:31, 3], ALU.add).then_inc(sc_used.sem, 1)
                    dve.wait_ge(sc_used.sem, sc_used.at(it, SC_IMP + 1))
                    V.tensor_tensor(sc_b, sc_a, const["forced"][:], ALU.add).then_inc(order.sem, 1)
                    dve.wait_ge(order.sem, order.next())
                    dve.sem_inc(waits_taken_dve, 1)
                    V.max(top, sc_b).then_inc(order.sem, 1)
                    dve.wait_ge(order.sem, order.next())
                    dve.sem_inc(waits_taken_dve, 1)
                    V.match_replace(sc_c, top, sc_b, NEG).then_inc(order.sem, 1)
                    dve.wait_ge(order.sem, order.next())
                    dve.sem_inc(waits_taken_dve, 1)
                    V.max(top, sc_c).then_inc(order.sem, 1)
                    dve.wait_ge(order.sem, order.next())
                    dve.sem_inc(waits_taken_dve, 1)
                    V.match_replace(sc_b, top, sc_c, NEG).then_inc(order.sem, 1)
                    dve.wait_ge(order.sem, order.next())
                    V.tensor_scalar(stat[0:64, 32:64], sc_b[:, 0:32], NEG / 2, NEG, ALU.is_gt, ALU.mult).then_inc(
                        s_mask.sem, 1)
                    dve.wait_ge(td_full.sem, td_full.at(it, TD_PTC + 1))
                    V.tensor_copy(ptc, bank[TD_PTC % 2][:, 0:64]).then_inc(td_used.sem, 1)
                    dve.wait_ge(td_full.sem, td_full.at(it, TD_PTW + 1))
                    B = bank[TD_PTW % 2]
                    V.tensor_copy(ptw[:, 0:4, :].rearrange("p c r -> p (c r)"), B[:, 0:256])
                    V.tensor_copy(ptw[0:64, 4, :], B[0:64, 256:320]).then_inc(td_used.sem, 1)
                    dve.wait_ge(s_bm.sem, s_bm.at(it, 1))
                    for u in range(4):
                        cols = slice(u * 512, (u + 1) * 512)
                        dve.wait_ge(sc_full.sem, sc_full.at(it, SC_SEL + u + 1))
                        dve.sem_inc(waits_taken_dve, 1)
                        negated(s_sel[:, cols], bank[2 + (SC_SEL + u) % 4][0:64, :], biasm[:, cols],
                                sm[0:64, 16 + u:17 + u]).then_inc(sc_used.sem, 1)
                    dve.wait_ge(sc_full.sem, sc_full.at(it, SC_SEL + 4 + 1))
                    new_scores(s_sel[:, PAST:PAST + 64], bank[2 + (SC_SEL + 4) % 4][0:64, 0:64],
                               const["nb_newa"][:, new], 20).then_inc(sc_used.sem, 1)
                    dve.wait_ge(sc_used.sem, sc_used.at(it, SC_SEL + 5))
                    V.tensor_reduce(stat[0:64, 27:28], sm[0:64, 16:21], X, ALU.min).then_inc(s_max.sem, 1)
                    dve.wait_ge(td_full.sem, td_full.at(it, TD_PTD + 1))
                    B = bank[TD_PTD % 2]
                    V.tensor_copy(ptd[:, 0:3, :].rearrange("p e r -> p (e r)"), B[:, 0:192])
                    V.tensor_copy(ptd[0:64, 3, :], B[0:64, 192:256]).then_inc(td_used.sem, 1)
                    dve.wait_ge(s_exp.sem, s_exp.at(it, EX_DIL))
                    V.reciprocal(sm[0:64, 15:16], stat[0:64, 30:31]).then_inc(order.sem, 1)
                    dve.wait_ge(order.sem, order.next())
                    V.tensor_scalar(diag[:, 192:256], ident[0:64, 0:64], sm[0:64, 15:16], None, ALU.mult).then_inc(
                        s_diag.sem, 1)
                    dve.wait_ge(sc_full.sem, sc_full.at(it, SC_WBD + 1))
                    V.tensor_copy(wb[:, 192:256], bank[2 + SC_WBD % 4][:, 0:64]).then_inc(sc_used.sem, 1)
                    dve.wait_ge(sc_used.sem, sc_used.at(it, SC_WBD + 1))
                    dve.wait_ge(od_full.sem, od_full.at(it, 1))
                    for k in range(2):
                        rows = slice(64 * k, 64 * k + 64)
                        V.tensor_tensor(
                            hT[rows, 4:8, put], bank[7][rows, 0:64].rearrange("p (q t h) -> p h q t", q=4, h=2)[:, k],
                            wb[rows, 192:256].rearrange("p (t q h) -> p h q t", t=8, h=2)[:, k], ALU.mult).then_inc(
                                out_put.sem, 1)
                    for u in range(3):
                        dve.wait_ge(td_full.sem, td_full.at(it, TD_PTS + u + 1))
                        B = bank[(TD_PTS + u) % 2]
                        if u < 2:
                            last = V.tensor_copy(pts[:, 8 * u:8 * u + 8, :].rearrange("p c r -> p (c r)"), B[:])
                        else:
                            last = V.tensor_copy(pts[0:64, 16, :], B[0:64, 0:64])
                        last.then_inc(td_used.sem, 1)
                    dve.wait_ge(s_exp.sem, s_exp.at(it, EX_SEL))
                    V.reciprocal(sm[0:64, 9:13], stat[0:64, 28:32]).then_inc(order.sem, 1)
                    dve.wait_ge(order.sem, order.next())
                    V.tensor_tensor(sm[0:64, 26:27], sm[0:64, 9:10], sgate[:, ds(b, 1), 0], ALU.mult).then_inc(
                        order.sem, 1)
                    dve.wait_ge(order.sem, order.next())
                    V.tensor_tensor(sm[0:64, 27:28], sm[0:64, 12:13], sgate[:, ds(b, 1), 1], ALU.mult)
                    V.tensor_tensor(sm[0:64, 28:29], sm[0:64, 10:11], sgate[:, ds(b, 1), 2], ALU.mult).then_inc(
                        order.sem, 1)
                    dve.wait_ge(order.sem, order.next())
                    V.tensor_tensor(
                        diag[:, 0:192].rearrange("p (e r) -> p e r", e=3),
                        ident[0:64, 0:64].unsqueeze(1).to_broadcast([64, 3, 64]),
                        sm[0:64, 26:29].unsqueeze(2).to_broadcast([64, 3, 64]), ALU.mult).then_inc(s_diag.sem, 1)
                    dve.wait_ge(sc_full.sem, sc_full.at(it, SC_WBA + 1))
                    V.tensor_copy(wb[:, 0:192], bank[2 + SC_WBA % 4][:, 0:192]).then_inc(sc_used.sem, 1)
                    dve.wait_ge(sc_used.sem, sc_used.at(it, SC_WBA + 1))
                    dve.wait_ge(oa_full.sem, oa_full.at(it, 1))
                    V.tensor_tensor(prod, bank[6][:, 0:192], wb[:, 0:192], ALU.mult).then_inc(order.sem, 1)
                    dve.wait_ge(order.sem, order.next())
                    for k in range(2):
                        rows = slice(64 * k, 64 * k + 64)
                        V.tensor_reduce(
                            hT[rows, 0:4, put], prod[rows, :].rearrange("p (e k g t) -> p k g t e", e=3, k=2, g=4)[:, k],
                            X, ALU.add).then_inc(out_put.sem, 1)
                if order.k != CH_S or lay.k != CH_L:
                    raise ValueError((order.k, lay.k))

                for n in range(2 * NT):
                    half, t = n // NT, n % NT
                    v = x[0:ROWS[t], t, half * CH:(half + 1) * CH]
                    dve.wait_ge(y_mm.sem, y_mm.at(l, n + 1))
                    V.tensor_tensor(v, v, bank[t][0:ROWS[t], :], ALU.add).then_inc(y_add.sem, 1)
                norm_keep(l * 2 + 1, 1)
                for n in range(2 * NT):
                    half, t = n // NT, n % NT
                    v = x[0:ROWS[t], t, half * CH:(half + 1) * CH]
                    dve.wait_ge(d_mm.sem, d_mm.at(l, n + 1))
                    V.tensor_tensor(v, v, bank[t][0:ROWS[t], :], ALU.add).then_inc(d_add.sem, 1)
            dve.wait_ge(rstd.sem, rstd.at(2 * DEPTH, 2))
            dve.wait_ge(c_ld.sem, c_ld.at(0, len(const) + 2))
            for t in range(NT):
                R = ROWS[t]
                V.scalar_tensor_tensor(x[0:R, t, :], x[0:R, t, :], stat[0:R, 8 + t:9 + t], gfin[0:R, :],
                                       ALU.mult, ALU.mult).then_inc(fin.sem, 1)


def laid_out(inputs):
    a = {n: np.asarray(v) for n, v in inputs.items()}
    put = {n: a[n] for n in ("x_prompt", "x_sample", "page_table", "w_in", "w_up", "w_down", "norm_final")}
    for n in ("norm_attn", "norm_mlp"):
        put[n] = a[n].reshape(DEPTH, KT, P).transpose(0, 2, 1)
    put["cmp_pe"] = a["cmp_pe"].reshape(DEPTH, 2, 16, 2, HD).transpose(0, 3, 4, 1, 2).reshape(DEPTH, P, 32)
    put["cmp_w1"] = a["cmp_w1"].reshape(DEPTH, 2, 16, 2, HD, 128).transpose(0, 3, 4, 1, 2, 5).reshape(DEPTH, P, -1)
    put["cmp_w2"] = a["cmp_w2"].transpose(0, 2, 1, 3).reshape(DEPTH, P, -1)
    w = a["w_out"]
    sparse = w[:, 0:512].reshape(DEPTH, 2, 4, HD, D).transpose(0, 2, 1, 3, 4).reshape(DEPTH, 512, D)
    put["w_out"] = np.concatenate([sparse, w[:, 512:]], 1)
    put["cache_kv_cmp"] = a["cache_kv_cmp"].reshape(DEPTH, POOL, 8, 8, 2, 2, 2, HD).transpose(
        0, 1, 4, 7, 5, 6, 3, 2).reshape(DEPTH, POOL, P, 256)

    def kt_and_v(rows):
        k, v = rows[..., 0, :, :], rows[..., 1, :, :]
        k = k.reshape(k.shape[:-2] + (P,))
        v = v.reshape(v.shape[:-2] + (P,))
        return np.concatenate([np.swapaxes(k, -1, -2), v], -1)

    put["cache_kv_sel"] = kt_and_v(a["cache_kv_sel"])
    win = a["state_kv_win"]
    put["window_tiles"] = kt_and_v(win.reshape(DEPTH, NB, 4, P, 2, 2, HD)).transpose(0, 1, 3, 2, 4)
    put["state_kv_win"] = win.reshape(DEPTH, NB, WIN, 256)
    dil = a["state_kv_dil"]
    put["state_kv_dil"] = dil.reshape(DEPTH, NB, PAST, D)
    by4 = dil[:, :, PAST - 4 * P:].reshape(DEPTH, NB, P, 4, 2, 8, HD)
    by16 = dil.reshape(DEPTH, NB, P, 16, 2, 8, HD)[:, :, :, 0:8]
    tiles = np.concatenate([dil[:, :, PAST - P:, None], by4, by16], 3)
    put["dilated_v"] = tiles[..., 1, :, :].reshape(DEPTH, NB, P, ND_TILES, CH)
    put["dilated_k"] = tiles[..., 0, :, :].reshape(DEPTH, NB, P, ND_TILES, 4, 2, HD).transpose(
        0, 1, 5, 6, 3, 4, 2).reshape(DEPTH, NB, P, ND_TILES, CH)
    return {n: np.ascontiguousarray(v) for n, v in put.items()}


OUT_SHAPES = {
    "y_p": (1, SEQ, D), "y_s": (NB, NS, D), "cmp_p": (DEPTH, 1, SEQ, 256), "sel_p": (DEPTH, 1, SEQ, 256),
    "win_p": (DEPTH, 1, SEQ, 256), "dil_p": (DEPTH, 1, SEQ, 1024), "cmp_s": (DEPTH, NB, NS, 256),
    "sel_s": (DEPTH, NB, NS, 256), "win_s": (DEPTH, NB, WIN, 256), "dil_s": (DEPTH, NB, PAST, 1024)}


def kernel(**inputs):
    import concourse.bacc as bacc
    from concourse.bass_utils import run_bass_kernel_spmd

    nc = bacc.Bacc("TRN2", target_bir_lowering=False, num_devices=1)
    arrays = laid_out(inputs)
    arrays.update(shape_constants())
    i = {n: nc.dram_tensor(f"in_{n}", a.shape, mybir.dt.from_np(a.dtype), kind="ExternalInput").ap()
         for n, a in arrays.items()}
    o = {n: nc.dram_tensor(f"out_{n}", shape, F32, kind="ExternalOutput").ap() for n, shape in OUT_SHAPES.items()}
    build(nc, i, o)
    r = run_bass_kernel_spmd(nc, [{f"in_{n}": a for n, a in arrays.items()}], core_ids=[0]).results[0]
    got = []
    for n, shape in OUT_SHAPES.items():
        heads = {"cmp": 2, "sel": 2, "win": 2, "dil": 8}.get(n[:3])
        a = r[f"out_{n}"]
        got.append(a.reshape(shape[:-1] + (2, heads, HD)) if heads else a)
    return tuple(got)
```

```python
from contextlib import ExitStack

import concourse.bass as bass
import numpy as np
from concourse import mybir

F32 = mybir.dt.float32
I32 = mybir.dt.int32
ALU = mybir.AluOpType
ACT = mybir.ActivationFunctionType
X = mybir.AxisListType.X
ds = bass.ds

P = 128
D = 1024
KT = D // P
DEPTH = 2
SEQ = 512
NB, NS = 8, 8
ROWS_S = NB * NS
PAST = 2048
PAGE = 128
NPG = PAST // PAGE
POOL = 160
HD = 64
NT = 5
ROWS = [P, P, P, P, ROWS_S]
TOK = SEQ + ROWS_S
DFF = 4096
CH = 512
EPS = 1e-6
NEG = -1e30
FORCE = 1e9
WIN = 512
SCALE = HD ** -0.5
NCK_P, NCK_S = SEQ // 16, PAST // 16
BIG = 3.0e38

Z_CHUNKS = [("qa", 0, 512), ("cs", 512, 1024), ("wg", 1024, 1304), ("qb", 1304, 1816),
            ("kb", 1816, 2328), ("vb", 2328, 2840)]
Z_STORES = {"qa": 0, "cs": 2, "wg": 1, "qb": 0, "kb": 1, "vb": 1}
NZ = len(Z_CHUNKS) * NT
NZT = 5 * NT
FIRST = ("ident", "mhalf")
STG = 4
W_OUT0, W_UP0, W_DN0, W_ALL = 6, 8, 16, 24

STEPS_A, STEPS_D = 24, 8
STEPS, ROUNDS = STEPS_A + STEPS_D, 4
AHEAD = 4
STEPS_L = ROUNDS * STEPS

TD_SD, TD_PTC, TD_PTW, TD_PTD, TD_PTS, TD_N = 0, 1, 2, 3, 4, 7
SC_HID, SC_KTC, SC_VC, SC_S, SC_WIN, SC_NEW, SC_IMP, SC_SEL, SC_DT, SC_WBA, SC_N = (
    0, 2, 3, 4, 5, 6, 7, 8, 12, 13, 14)
EX_CMP, EX_WIN, EX_DIL, EX_SEL = 1, 2, 3, 4
ND_TILES, ND_A = 13, 5


CH_L, CH_A, CH_S = 6, ROUNDS * (2 * STEPS_A + STEPS_D), 20


def step_keys(m):
    if m < STEPS_A and m % 12 < 4:
        return NCK_P
    return (m % 4 + 1) * P


def constants():
    f = np.float32
    slopes = np.exp2(-8.0 * np.arange(1, 17) / 16).astype(f)
    c = {}
    p = np.arange(P)[:, None]
    x = np.arange(SEQ)[None] - 384
    dist = p - x
    c["nd"] = np.where(dist >= 0, -dist, NEG).astype(f)
    n = (dist <= 128).astype(int) + (dist % 4 == 0) + (dist % 16 == 0)
    c["lnb"] = np.where(n > 0, np.log(np.maximum(n, 1)), NEG).astype(f)
    t = (np.arange(4)[None, :, None] * P + np.arange(P)[:, None, None])
    dc = t - (np.arange(32)[None, None] * 16 + 31)
    c["ndc"] = np.where((dc >= 0) & (np.arange(32) < 31), -dc, NEG).astype(f).reshape(P, 128)
    c["okrow"] = (np.arange(P)[:, None] >= 31).astype(f)
    c["mhalf"] = np.full((P, NT), -0.5, f)
    c["slopes"] = np.tile(slopes[None], (P, 1))
    c["ident"] = np.eye(P, dtype=f)
    c["half"] = (np.arange(P)[:, None] // HD == np.arange(2)[None]).astype(f)
    r = np.arange(64)
    sa, ta = slopes[0::2][r // 8][:, None], (r % 8)[:, None]
    rd = np.arange(P)
    sd, td = slopes[1::2][rd % 8][:, None], (rd // 32 + rd // 8 % 2 * 4)[:, None]
    pos = np.arange(PAST)[None]
    c["b_sel"] = (-sa * (PAST + ta - pos)).astype(f)
    w = np.arange(WIN)[None]
    rel = WIN + ta - w
    c["b_win"] = np.where(rel < WIN, -sa * rel, NEG).astype(f)
    k = np.arange(128)[None]
    c["b_cmp"] = np.where(k < 127, -sa * (PAST + ta - 16 * k - 31), NEG).astype(f)
    b = np.arange(NB)[None, :, None]
    b2, t2 = (r // 8)[None, None], (r % 8)[None, None]
    ok = (b == b2) & (t2 <= ta[:, :, None])
    c["nb_newa"] = -np.where(ok, -sa[:, :, None] * (ta[:, :, None] - t2), NEG).astype(f).reshape(64, 512)
    dd = td[:, :, None] - t2
    nn = 1 + (dd % 4 == 0) + (dd == 0)
    okd = (b == b2) & (dd >= 0)
    void = (rd % 32 // 8 == 2)[:, None]
    c["nb_newd"] = -np.where(okd, -sd[:, :, None] * dd + np.log(nn), NEG).astype(f).reshape(P, 512)
    d1 = np.where(k >= td, -sd * (128 + td - k), NEG)
    d4 = PAST + td - (1536 + 4 * k + td % 4)
    d2 = np.where(d4 <= 512, -sd * d4, NEG)
    d3 = np.where(void, NEG, -sd * (PAST - 16 * k))
    c["b_dil"] = np.concatenate([d1, d2, d3], 1).astype(f)
    c["own_head"] = (rd[:, None] % 8 == np.arange(8)[None]).astype(f)
    c["own_step"] = ((td == np.arange(8)[None]) & (rd[:, None] % 32 < 16)).astype(f)
    forced = np.zeros((64, 33), f)
    forced[:, [0, 31, 32]] = FORCE
    c["forced"] = forced
    same = (r[:, None] // 32 == r[None] // 32) & (r[:, None] % 8 == r[None] % 8)
    c["gsum"] = same.astype(f)
    c["ones"] = np.ones((64, 128), f)
    c["tsel"] = (r[:, None] % 8 == r[None] % 8).astype(f)
    c["bsel"] = (r[:, None] // 8 == np.arange(8)[None]).astype(f)
    c["hsel"] = np.tile((r[:, None] // 8 == np.arange(8)[None])[:, None, :, None], (1, 8, 1, 3)
                        ).astype(f).reshape(64, 192)
    return c


def shape_constants():
    c = constants()
    rest = [np.pad(a, ((0, P - a.shape[0]), (0, 0))) for n, a in c.items() if n not in FIRST]
    return {**{n: c[n] for n in FIRST}, "constants": np.concatenate(rest, 1)}


class Count:

    def __init__(self, ctx, nc, name, per, unit=1):
        self.sem, self.per, self.unit = ctx.enter_context(nc.semaphore(name)), per, unit

    def at(self, i, k):
        return i * (self.per * self.unit) + (k * self.unit + 1)


def build(nc, i, o):
    ctx = ExitStack()
    with ctx:
        def sb(name, *shape, dt=F32):
            return ctx.enter_context(nc.sbuf_tensor(name, list(shape), dt))

        def load_sem(name, per):
            return Count(ctx, nc, name, per, 16)

        def ev(name, per):
            return Count(ctx, nc, name, per)

        const = {n: sb("c_" + n, *a.shape) for n, a in constants().items() if n in FIRST}
        packed, at = sb("constants", *shape_constants()["constants"].shape), 0
        for n, a in constants().items():
            if n not in FIRST:
                const[n] = packed[0:a.shape[0], at:at + a.shape[1]]
                at += a.shape[1]
        ident, slopes = const["ident"], const["slopes"]
        x = sb("x", P, NT, D)
        hT = sb("hT", P, KT, TOK)
        gain = sb("gain", P, 2, KT)
        w1 = sb("w1", P, 2, 16, 128)
        w2 = sb("w2", P, 2, HD)
        pe_in = sb("pe_in", P, 2, 16)
        cbias = sb("cbias", P, 2)
        ncbias = sb("ncbias", P, 2)
        gate = sb("gate", P, NT, 24)
        sgate = sb("sgate", 64, NB, 3)
        ktcp = sb("ktcp", P, NCK_P)
        vcp = sb("vcp", NCK_P, 128)
        qd = sb("qd", P, NB, 64)
        qdb = sb("qdb", P, 4, NB, NS, 2)
        kns, knw = sb("kns", P, 64), sb("knw", P, 64)
        knb = sb("knb", P, 4, 64)
        vsm = sb("vsm", 64, 768)
        stat = sb("stat", P, 64)
        sm = sb("sm", P, 64)
        topk = sb("topk", 64, 33 * 3 + 8)
        gs = sb("gs", 64, 64)
        q_s = sb("q_s", P, 64)
        pages = sb("pages", 1, NB * NPG, dt=I32)
        ring = sb("ring", P, 2, KT * CH)
        zone = sb("zone", P, 21900)

        def part(at, *shape, rows=slice(0, P)):
            n = int(np.prod(shape))
            v = zone[rows, at:at + n]
            if len(shape) == 1:
                return v
            names = "abcd"[:len(shape)]
            return v.rearrange(f"p ({' '.join(names)}) -> p {' '.join(names)}",
                               **dict(zip(names[1:], shape[1:])))

        qaT, qbT, kbT = part(0, 4, SEQ), part(2048, 4, SEQ), part(4096, 4, SEQ)
        ksT, kwT = part(6144, SEQ), part(6656, SEQ)
        vst = part(7168, 4, 768)
        og = part(10240, 4, 128)
        W = 11328
        xn = part(W, 2, D)
        p_bias, p_biasc = part(W, 2, SEQ), part(W + 1024, 2, 128)
        p_sb = part(W + 1280, 4, SEQ)
        p_pt = part(W + 3328, 2, SEQ)
        p_q = [part(W + 4352, SEQ), part(10752, SEQ)]
        p_k = part(W + 4864, SEQ)
        p_qd = [part(W + 5376, SEQ), part(W + 7424, SEQ)]
        p_biasd = part(W + 5888, 2, SEQ)
        ogd = part(W + 6912, 4, 128)
        stg_at = W + 8100
        stg = part(stg_at, STG, CH)
        vd = part(0, ND_TILES, CH)
        kda, kdb = part(6656, ND_A, CH), part(9216, 4, CH)
        relaid = [part(W, 2048), part(W + 6016, 2048)]
        xt = [part(W + 2048 + s * 768, 3, 8, NCK_P) for s in range(2)]
        biasm = part(W, 2048, rows=slice(0, 64))
        s_sel = part(W + 2048, 2112, rows=slice(0, 64))
        pts = part(W + 4160, 17, 64)
        m = W + 5248
        he, hid = part(m, 256), part(m + 256, 2, 256)
        ktc, vc = part(m + 768, 128), part(m + 896, 128)
        s_c = part(m + 1024, 128, rows=slice(0, 64))
        ptc = part(m + 1152, 64)
        s_win = part(m + 1216, 576, rows=slice(0, 64))
        s_d = part(m + 2048, 448)
        d_own = part(m + 1792, 512)
        diag = part(m + 2496, 256, rows=slice(0, 64))
        kw_sb = part(stg_at, 4, 256)
        ptw = part(stg_at + 1024, 5, 64)
        ptd = part(stg_at + 1344, 4, P)
        wb = part(stg_at + 1856, 192)
        prod = part(stg_at + 2048, 192)
        strips = part(W, 3, 520)
        gb, gm = diag[:, 0:192], part(m + 2048, 192, rows=slice(0, 64))
        uT = part(0, 32, TOK)
        assert m + 2752 <= stg_at and stg_at + 2240 <= 21900
        gfin = part(W + 4096, D)
        raw = ring[:, 0, :]
        rawt = raw.rearrange("p (g s k i n) -> p g s k i n", g=NPG, s=2, k=2, i=8)
        kvsel = ring[:, 1, :].rearrange("p (g f) -> p g f", g=NPG)

        bank = [ctx.enter_context(nc.psum_tensor(f"bank{n}", [P, 512], F32)) for n in range(8)]

        first_ld, c_ld = load_sem("first_constants_loaded", 0), load_sem("constants_loaded", 0)
        gfin_ld = load_sem("final_gain_loaded", 0)
        x_ld = load_sem("rows_loaded", 0)
        gain_ld, comp_ld = load_sem("gains_loaded", 2), load_sem("compression_loaded", 3)
        w_ld = [load_sem(f"weights_loaded{n}", W_ALL // 2) for n in range(2)]
        copies = load_sem("state_copied", 0)
        sq = ev("squares_summed", NT)
        rstd = ev("rstd_ready", 2)
        xn_rdy = ev("normed", NT)
        n_tr = ev("normed_transposed", 2 * NT)
        h_rdy = ev("hT_ready", 2 * NT)
        z_mm = ev("z_products", NZ)
        z_stg = ev("z_staged", NZ)
        z_tr = ev("z_transposed", NZT)
        z_te = ev("z_transposed_kept", NZT)
        z_v = ev("z_values_kept", 3 * NT)
        g_exp = ev("gates_exp", NT)
        g_rdy = ev("gates_ready", 2)
        slot_n = [0] * STG
        store_at = {}
        for n in range(NZ):
            slot_n[n % STG] += Z_STORES[Z_CHUNKS[n // NT][0]]
            store_at[n] = slot_n[n % STG]
        z_out = [load_sem(f"z_stored{s}", slot_n[s]) for s in range(STG)]
        sg_mm, sg_rdy = ev("sample_gates_product", 1), ev("sample_gates", 3)
        raw_p = load_sem("prompt_chunks_loaded", 4)
        raw_ld = load_sem("raw_loaded", NPG)
        cleared = ev("cleared", 0)
        pb_rdy = ev("compress_bias", 2)
        ct_p, xt_p = ev("prompt_chunks_transposed", 8), ev("prompt_chunks_kept", 8)
        hid_p, hexp_p, hdone_p = ev("prompt_hidden", 2), ev("prompt_hidden_exp", 2), ev("prompt_hidden_done", 2)
        kvc_p, kvc_pk = ev("prompt_compressed", 2), ev("prompt_compressed_kept", 2)
        a_s, a_sb, a_e = ev("scores", STEPS_L), ev("scores_biased", STEPS_L), ev("probs", STEPS_L)
        a_t, a_pt, a_o = ev("probs_transposed", STEPS_L), ev("probsT_kept", STEPS_L), ev("outputs", STEPS_L)
        a_acc = ev("outputs_added", STEPS_L)
        a_bias = ev("head_bias", 8)
        a_q = ev("pair_queries", 8)
        s_q, s_clear = ev("batch_queries", 1), ev("query_strips_cleared", 1)
        og_t, og_k = ev("pair_transposed", 8), ev("pair_kept", 8)
        sel_ld, win_ld = load_sem("selected_loaded", NPG), load_sem("window_loaded", 1)
        kda_ld, kdb_ld = load_sem("dilated_ka_loaded", 2), load_sem("dilated_kb_loaded", 1)
        vd_ld = load_sem("dilated_v_loaded", 1)
        td_full, td_used = ev("bank01_full", TD_N), ev("bank01_used", TD_N)
        sc_full, sc_used = ev("banks2to5_full", SC_N), ev("banks2to5_used", SC_N)
        s_hexp = ev("hidden_exp", 2)
        s_exp = ev("sample_probs", 4)
        s_max = ev("sample_max", 2)
        s_bm = ev("selection_bias", 1)
        s_mask = ev("selection_mask", 1)
        s_gs = ev("group_sums_scaled", 1)
        s_diag, d_scaled = ev("weights_diagonal", 1), ev("dilated_out_scaled", 1)
        oa_full, od_full = ev("sparse_out", 1), ev("dilated_out", 1)
        out_put = ev("sample_out_kept", 2)
        win_pv = ev("window_out", 1)
        kda_used = ev("dilated_ka_used", 1)
        ch_l, ch_a, ch_s = ev("vector_order_layer", CH_L), ev("vector_order_prompt", CH_A), ev("vector_order_batch", CH_S)
        y_mm, y_add = ev("y_products", 2 * NT), ev("y_added", 2 * NT)
        u_mm, u_relu, u_sq = ev("u_products", 32), ev("u_relu", 32), ev("u_squared", 32)
        d_mm, d_add = ev("down_products", 2 * NT), ev("down_added", 2 * NT)
        d_chunk = ev("down_chunks", 6)
        fin, fin_out = ev("final_rows", NT), [load_sem(f"final_stored{n}", 1) for n in range(2)]
        win_out = load_sem("window_state_stored", 0)
        waits_taken_sp, waits_taken_pool, waits_taken_pe, waits_taken_dve = (
            ctx.enter_context(nc.semaphore(f"waits_taken_{e}")) for e in ("sp", "pool", "pe", "dve"))
        by_engine = {
            "sync": [first_ld, gfin_ld, x_ld, gain_ld, comp_ld, *w_ld, copies, raw_p, raw_ld, sel_ld,
                     win_ld, kda_ld, kdb_ld, vd_ld, win_out],
            "scalar": [c_ld, sq, xn_rdy, z_stg, g_exp, hexp_p, a_e, a_pt, s_hexp, s_exp, u_relu, *z_out, *fin_out],
            "gpsimd": [rstd, z_v, s_bm, u_sq, a_q, s_q, s_clear],
            "tensor": [n_tr, z_mm, z_tr, sg_mm, ct_p, hid_p, kvc_p, a_s, a_t, a_o, og_t, td_full,
                       sc_full, oa_full, od_full, y_mm, u_mm, d_mm, d_chunk, win_pv, kda_used],
            "vector": [cleared, h_rdy, z_te, g_rdy, sg_rdy, pb_rdy, xt_p, hdone_p, kvc_pk, a_sb, a_acc, a_bias, og_k,
                       td_used, sc_used, s_max, s_mask, s_gs, s_diag, d_scaled, out_put, ch_l, ch_a, ch_s, y_add, d_add, fin],
        }

        def begin(eng, name):
            for c in by_engine[name]:
                eng.sem_inc(c.sem, 1)

        block = ctx.enter_context(nc.Block())

        def z_kind(n):
            return Z_CHUNKS[n // NT][0], n % NT

        def a_step(s):
            return s // 12, s % 12 // 4, s % 4

        def in_round(g, m):
            return (g + 1, m - STEPS) if m >= STEPS else (g, m)

        @block.sync
        def _(sp):
            begin(sp, "sync")

            for n in FIRST:
                sp.dma_start(const[n][:], i[n]).then_inc(first_ld.sem, 16)
            sp.dma_start(x[:, 0:4, :], i["x_prompt"][0].rearrange("(t p) d -> p t d", p=P)).then_inc(x_ld.sem, 16)
            sp.dma_start(x[0:64, 4, :], i["x_sample"].rearrange("b t d -> (b t) d")).then_inc(x_ld.sem, 16)

            def wait_used(l, n):
                if n == -2:
                    sp.wait_ge(d_chunk.sem, d_chunk.at(l, 0))
                elif n == -1:
                    sp.wait_ge(d_mm.sem, d_mm.at(l, 0))
                elif n < W_OUT0:
                    sp.wait_ge(z_mm.sem, z_mm.at(l, NT * (n + 1)))
                elif n < W_UP0:
                    sp.wait_ge(y_mm.sem, y_mm.at(l, NT * (n - W_OUT0 + 1)))
                elif n < W_DN0:
                    sp.wait_ge(u_mm.sem, u_mm.at(l, 4 * (n - W_UP0 + 1)))
                elif (n - W_DN0) % 4 == 3:
                    sp.wait_ge(d_mm.sem, d_mm.at(l, NT * ((n - W_DN0) // 4 + 1)))
                else:
                    sp.wait_ge(d_chunk.sem, d_chunk.at(l, (n - W_DN0) // 4 * 3 + (n - W_DN0) % 4 + 1))

            with sp.Fori(0, DEPTH) as l:
                L = ds(l, 1)

                def chunk(n, src):
                    wait_used(l, n - 2)
                    width = src.shape[-1]
                    dst = ring[:, n % 2, :].rearrange("p (k c) -> p k c", k=KT)[:, :, 0:width]
                    sp.dma_start(dst, src).then_inc(w_ld[n % 2].sem, 16)
                    copy_state(n)

                def copy_state(n):
                    b, r = n // 3, n % 3
                    rows = (PAST - NS) // 3
                    sp.dma_start(
                        o["dil_s"][L, b, r * rows:(r + 1) * rows].rearrange("o r f -> (o r) f"),
                        i["state_kv_dil"][L, b, NS + r * rows:NS + (r + 1) * rows].rearrange("o r f -> (o r) f")).then_inc(
                            copies.sem, 16)

                def load_prompt_chunks():
                    for t in range(4):
                        n = NT + t
                        sp.wait_ge(z_out[n % STG].sem, z_out[n % STG].at(l, store_at[n]))
                        sp.sem_inc(waits_taken_sp, 1)
                    src = o["cmp_p"][L, 0].rearrange("o (n c) (s k d) -> s k (o n) c d", c=16, s=2, k=2)
                    for s in range(2):
                        for k in range(2):
                            dst = relaid[s][0:NCK_P, k * 1024:(k + 1) * 1024].rearrange("p (c d) -> p c d", c=16)
                            sp.dma_start(dst, src[s, k]).then_inc(raw_p.sem, 16)

                wait_used(l, -1)
                sp.dma_start(gain[:, 0, :], i["norm_attn"][L].rearrange("o p k -> (o p) k")).then_inc(gain_ld.sem, 16)
                sp.dma_start(gain[:, 1, :], i["norm_mlp"][L].rearrange("o p k -> (o p) k")).then_inc(gain_ld.sem, 16)
                for n, (_, a, z) in enumerate(Z_CHUNKS):
                    if n == 4:
                        load_prompt_chunks()
                    chunk(n, i["w_in"][L, :, a:z].rearrange("o (k p) c -> p (o k) c", p=P))
                    if n == 0:
                        sp.dma_start(pe_in[:].rearrange("p s i -> p (s i)"),
                                     i["cmp_pe"][L].rearrange("o p f -> (o p) f")).then_inc(comp_ld.sem, 16)
                        sp.dma_start(w1[:].rearrange("p s i h -> p (s i h)"),
                                     i["cmp_w1"][L].rearrange("o p f -> (o p) f")).then_inc(comp_ld.sem, 16)
                        sp.dma_start(w2[:].rearrange("p s d -> p (s d)"),
                                     i["cmp_w2"][L].rearrange("o p f -> (o p) f")).then_inc(comp_ld.sem, 16)
                        for b in range(NB):
                            sp.dma_start(
                                o["win_s"][L, b, 0:WIN - NS].rearrange("o r f -> (o r) f"),
                                i["state_kv_win"][L, b, NS:WIN].rearrange("o r f -> (o r) f")).then_inc(
                                    win_out.sem, 16)

                def page_rows(b, cache, dst, sem):
                    for g in range(NPG):
                        page = sp.value_load(pages[0:1, ds(b * NPG + g, 1)], min_val=0, max_val=POOL - 1)
                        sp.dma_start(dst[:, g, :], i[cache][L, ds(page, 1)].rearrange("o q p f -> (o q p) f")).then_inc(
                            sem.sem, 16)

                def of_batch(name, b):
                    return i[name][L, ds(b, 1)].rearrange("o q p g f -> (o q p) g f")

                def load_raw(b):
                    page_rows(b, "cache_kv_cmp", raw.rearrange("p (g f) -> p g f", g=NPG), raw_ld)

                def load_selected(b):
                    page_rows(b, "cache_kv_sel", kvsel, sel_ld)

                def load_window(b):
                    sp.dma_start(kw_sb, of_batch("window_tiles", b)).then_inc(win_ld.sem, 16)

                def load_dilated_k(b):
                    sp.dma_start(kda, of_batch("dilated_k", b)[:, 0:ND_A, :]).then_inc(kda_ld.sem, 16)
                    sp.dma_start(kdb, of_batch("dilated_k", b)[:, ND_A:ND_A + 4, :]).then_inc(kdb_ld.sem, 16)

                def load_dilated_k_rest(b):
                    sp.wait_ge(kda_used.sem, kda_used.at(l * NB + b, 1))
                    sp.dma_start(kda[:, 0:4, :], of_batch("dilated_k", b)[:, ND_A + 4:, :]).then_inc(kda_ld.sem, 16)

                def load_dilated_v(b):
                    sp.dma_start(vd, of_batch("dilated_v", b)).then_inc(vd_ld.sem, 16)

                sp.wait_ge(c_ld.sem, c_ld.at(0, 2))
                wait_used(l, W_OUT0 - 2)
                sp.sem_inc(waits_taken_sp, 1)
                load_raw(0)
                wait_used(l, W_OUT0 - 1)
                sp.sem_inc(waits_taken_sp, 1)
                load_selected(0)
                for s in range(STG):
                    sp.wait_ge(z_out[s].sem, z_out[s].at(l, slot_n[s]))
                    sp.sem_inc(waits_taken_sp, 1)
                sp.wait_ge(z_v.sem, z_v.at(l, 3 * NT))
                sp.wait_ge(z_tr.sem, z_tr.at(l, NZT))
                load_window(0)
                sp.wait_ge(og_k.sem, og_k.at(l, 8))
                load_dilated_k(0)
                load_dilated_v(0)
                with sp.Fori(0, NB - 1) as b:
                    it = l * NB + b
                    load_dilated_k_rest(b)
                    load_raw(b + 1)
                    sp.wait_ge(td_full.sem, td_full.at(it, TD_SD + 1))
                    load_dilated_k(b + 1)
                    sp.wait_ge(win_pv.sem, win_pv.at(it, 1))
                    sp.wait_ge(od_full.sem, od_full.at(it, 1))
                    load_window(b + 1)
                    load_dilated_v(b + 1)
                    sp.wait_ge(oa_full.sem, oa_full.at(it, 1))
                    sp.sem_inc(waits_taken_sp, 1)
                    load_selected(b + 1)
                load_dilated_k_rest(NB - 1)

                for half in range(2):
                    n = W_OUT0 + half
                    if half == 0:
                        sp.wait_ge(sc_full.sem, sc_full.at(l * NB + NB - 1, SC_HID + 2))
                        sp.sem_inc(waits_taken_sp, 1)
                    else:
                        sp.wait_ge(oa_full.sem, oa_full.at(l * NB + NB - 1, 1))
                    chunk(n, i["w_out"][L, :, half * CH:(half + 1) * CH].rearrange("o (k p) c -> p (o k) c", p=P))
                for n in range(W_UP0, W_DN0):
                    c = n - W_UP0
                    chunk(n, i["w_up"][L, :, c * CH:(c + 1) * CH].rearrange("o (k p) c -> p (o k) c", p=P))
                for n in range(W_DN0, W_ALL):
                    half, c = (n - W_DN0) // 4, (n - W_DN0) % 4
                    chunk(n, i["w_down"][L, c * D:(c + 1) * D, half * CH:(half + 1) * CH].rearrange(
                        "o (k p) c -> p (o k) c", p=P))
            sp.wait_ge(d_mm.sem, d_mm.at(DEPTH - 1, 2 * NT))
            sp.dma_start(gfin, i["norm_final"].rearrange("(o d) -> o d", o=1).broadcast_to([P, D])).then_inc(
                gfin_ld.sem, 16)
            sp.wait_ge(copies.sem, copies.at(0, DEPTH * W_ALL))
            sp.wait_ge(win_out.sem, win_out.at(0, DEPTH * NB))

        @block.scalar
        def _(act):
            begin(act, "scalar")
            copy = nc.scalar.copy
            act.wait_ge(x_ld.sem, x_ld.at(0, 2))
            act.wait_ge(cleared.sem, cleared.at(0, 1))

            def values_before(n):
                return sum(z_kind(q)[0] in ("cs", "wg", "vb") for q in range(n))

            def squares(r, t):
                R = ROWS[t]
                nc.scalar.activation(part(stg_at, D)[0:R, :], x[0:R, t, :], ACT.Square,
                                     accum_out=stat[0:R, t:t + 1]).then_inc(sq.sem, 1)
                act.wait_ge(sq.sem, sq.at(r, t + 1))

            def norm_rows(r):
                act.wait_ge(rstd.sem, rstd.at(r, 2))
                for t in range(NT):
                    R = ROWS[t]
                    if t >= 2:
                        act.wait_ge(n_tr.sem, n_tr.at(r, 2 * (t - 1)))
                    nc.scalar.mul(xn[0:R, t % 2, :], x[0:R, t, :], stat[0:R, 8 + t:9 + t]).then_inc(xn_rdy.sem, 1)

            def out_rows(n, l):
                kind, t = z_kind(n)
                R, L = ROWS[t], ds(l, 1)
                s = stg[:, n % STG, :]

                def put(name, cols, lo=0, hi=None):
                    if t < 4:
                        dst = o[name + "_p"][L, 0, t * P:(t + 1) * P, lo:hi].rearrange("o r f -> (o r) f")
                    elif name in ("win", "dil"):
                        keep = (WIN if name == "win" else PAST) - NS
                        dst = o[name + "_s"][L, :, keep:keep + NS, lo:hi].rearrange("o b r f -> (o b) r f")
                    else:
                        dst = o[name + "_s"][L, :, :, lo:hi].rearrange("o b r f -> (o b) r f")
                    act.dma_start(dst, s[0:R, cols[0]:cols[1]]).then_inc(z_out[n % STG].sem, 16)
                if kind == "cs":
                    put("cmp", (0, 256), 0, 256)
                    put("sel", (256, 512), 0, 256)
                if kind == "wg":
                    put("win", (0, 256), 0, 256)
                if kind == "kb":
                    put("dil", (0, 512), 0, 512)
                if kind == "vb":
                    put("dil", (0, 512), 512, 1024)

            def project(l):
                for n in range(NZ):
                    kind, t = z_kind(n)
                    R = ROWS[t]
                    width = Z_CHUNKS[n // NT][2] - Z_CHUNKS[n // NT][1]
                    s, z = stg[0:R, n % STG, 0:width], bank[4 + n % 2][0:R, 0:width]
                    if n >= STG:
                        act.wait_ge(z_tr.sem, z_tr.at(l, min(n - STG + 1, NZT)))
                        act.wait_ge(z_v.sem, z_v.at(l, values_before(n - STG + 1)))
                        act.wait_ge(z_out[n % STG].sem, z_out[n % STG].at(l, store_at[n - STG]))
                    act.wait_ge(z_mm.sem, z_mm.at(l, n + 1))
                    if kind == "qa":
                        nc.scalar.activation(
                            s.rearrange("p (g k d) -> p k g d", g=4, k=2),
                            z.rearrange("p (k g d) -> p k g d", g=4, k=2), ACT.Copy, scale=SCALE).then_inc(
                                z_stg.sem, 1)
                    elif kind == "qb":
                        nc.scalar.activation(s, z, ACT.Copy, scale=SCALE).then_inc(z_stg.sem, 1)
                    else:
                        if kind == "wg":
                            nc.scalar.activation(gate[0:R, t, :], z[:, 256:280], ACT.Exp, scale=-1.0).then_inc(
                                g_exp.sem, 1)
                        copy(s, z).then_inc(z_stg.sem, 1)
                        act.wait_ge(z_stg.sem, z_stg.at(l, n + 1))
                        out_rows(n, l)

            def prompt_steps(l, g, first, last, ends):
                for m in range(first, last):
                    n = g * STEPS + m
                    if m < STEPS or not ends:
                        w = step_keys(m % STEPS)
                        act.wait_ge(a_sb.sem, a_sb.at(l, n + 1))
                        nc.scalar.activation(
                            p_sb[:, m % 4, 0:w], p_sb[:, m % 4, 0:w], ACT.Exp, scale=-1.0,
                            bias=stat[:, 16 + m % 4:17 + m % 4], accum_out=stat[:, 32 + m % 8:33 + m % 8]).then_inc(
                            a_e.sem, 1)
                    if m >= 2 and (m - 2 < STEPS or not ends):
                        w = step_keys((m - 2) % STEPS)
                        act.wait_ge(a_t.sem, a_t.at(l, n - 1))
                        if m >= 4:
                            act.wait_ge(a_o.sem, a_o.at(l, n - 3))
                        R, cols = (NCK_P, P) if w == NCK_P else (P, w)
                        copy(p_pt[0:R, m % 2, 0:cols], bank[2 + m % 2][0:R, 0:cols]).then_inc(a_pt.sem, 1)

            for t in range(NT):
                squares(0, t)
            act.dma_start(packed[:], i["constants"]).then_inc(c_ld.sem, 16)
            act.dma_start(pages[0:1, :], i["page_table"].rearrange("(o b) g -> o (b g)", o=1)).then_inc(c_ld.sem, 16)
            with act.Fori(0, DEPTH) as l:
                norm_rows(l * 2)
                project(l)
                for s in range(2):
                    act.wait_ge(pb_rdy.sem, pb_rdy.at(l, s + 1))
                    act.wait_ge(hid_p.sem, hid_p.at(l, s + 1))
                    act.wait_ge(hdone_p.sem, hdone_p.at(l, s))
                    nc.scalar.activation(he[:, 0:2 * NCK_P], bank[2 + s][:, 0:2 * NCK_P], ACT.Exp,
                                         scale=-1.0, bias=ncbias[:, s:s + 1]).then_inc(hexp_p.sem, 1)
                prompt_steps(l, 0, 0, AHEAD, False)
                with act.Fori(0, ROUNDS - 1) as g:
                    prompt_steps(l, g, AHEAD, STEPS + AHEAD, False)
                prompt_steps(l, ROUNDS - 1, AHEAD, STEPS + AHEAD, True)

                with act.Fori(0, NB) as b:
                    it = l * NB + b
                    for s in range(2):
                        act.wait_ge(sc_full.sem, sc_full.at(it, SC_HID + s + 1))
                        act.wait_ge(sc_used.sem, sc_used.at(it, SC_HID + s))
                        nc.scalar.activation(
                            he.rearrange("p (k n) -> p k n", k=2),
                            bank[2 + s][:, 0:258].rearrange("p (k n) -> p k n", k=2)[:, :, 1:129],
                            ACT.Exp, scale=-1.0, bias=ncbias[:, s:s + 1]).then_inc(s_hexp.sem, 1)

                    def probs(scores, n, R=64):
                        nc.scalar.activation(scores, scores, ACT.Exp, scale=-1.0, bias=stat[0:R, 23 + n:24 + n],
                                             accum_out=stat[0:R, 27 + n:28 + n]).then_inc(s_exp.sem, 1)
                    act.wait_ge(sc_used.sem, sc_used.at(it, SC_S + 1))
                    probs(s_c, EX_CMP)
                    act.wait_ge(s_max.sem, s_max.at(it, 1))
                    probs(s_win, EX_WIN)
                    act.wait_ge(td_used.sem, td_used.at(it, TD_SD + 1))
                    probs(s_d, EX_DIL, P)
                    act.wait_ge(s_max.sem, s_max.at(it, 2))
                    probs(s_sel, EX_SEL)

                for t in range(NT):
                    act.wait_ge(y_add.sem, y_add.at(l, NT + t + 1))
                    squares(l * 2 + 1, t)
                norm_rows(l * 2 + 1)
                with act.Fori(0, 8) as c:
                    for q in range(4):
                        f = c * 4 + q
                        act.wait_ge(u_mm.sem, u_mm.at(l, f + 1))
                        v = uT[:, ds(f, 1), :].rearrange("p o t -> p (o t)")
                        nc.scalar.activation(v[:, 0:TOK // 2], bank[2 * (q % 2)][:, 0:TOK // 2], ACT.Relu)
                        nc.scalar.activation(v[:, TOK // 2:TOK], bank[2 * (q % 2) + 1][:, 0:TOK // 2],
                                             ACT.Relu).then_inc(u_relu.sem, 1)
                for t in range(NT):
                    act.wait_ge(d_add.sem, d_add.at(l, NT + t + 1))
                    squares(l * 2 + 2, t)
            for t in range(NT):
                R = ROWS[t]
                act.wait_ge(fin.sem, fin.at(0, t + 1))
                dst = o["y_p"][0, t * P:(t + 1) * P, :] if t < 4 else o["y_s"].rearrange("b t d -> (b t) d")
                act.dma_start(dst, x[0:R, t, :]).then_inc(fin_out[t % 2].sem, 16)
            act.wait_ge(fin_out[0].sem, fin_out[0].at(0, 3))
            act.wait_ge(fin_out[1].sem, fin_out[1].at(0, 2))
            for s in range(STG):
                act.wait_ge(z_out[s].sem, z_out[s].at(DEPTH - 1, slot_n[s]))

        @block.gpsimd
        def _(pool):
            begin(pool, "gpsimd")

            def row_scale(r):
                pool.wait_ge(sq.sem, sq.at(r, NT))
                pool.sem_inc(waits_taken_pool, 1)
                nc.gpsimd.tensor_scalar(stat[:, 8:8 + NT], stat[:, 0:NT], 1.0 / D, EPS, ALU.mult, ALU.add).then_inc(
                    rstd.sem, 1)
                pool.wait_ge(rstd.sem, rstd.at(r, 1))
                nc.gpsimd.tensor_tensor(stat[:, 8:8 + NT], stat[:, 8:8 + NT], const["mhalf"][:], ALU.pow).then_inc(
                    rstd.sem, 1)

            pool.wait_ge(first_ld.sem, first_ld.at(0, len(FIRST)))
            with pool.Fori(0, DEPTH) as l:
                row_scale(l * 2)
                for n in range(NZ):
                    kind, t = z_kind(n)
                    if kind not in ("cs", "wg", "vb"):
                        continue
                    R = ROWS[t]
                    src, at, w = {"cs": (384, 0, 128), "wg": (128, 128, 128), "vb": (0, 256, 512)}[kind]
                    dst = vst[:, t, at:at + w] if t < 4 else vsm[:, at:at + w]
                    pool.wait_ge(z_stg.sem, z_stg.at(l, n + 1))
                    pool.sem_inc(waits_taken_pool, 1)
                    nc.gpsimd.tensor_copy(dst, stg[0:R, n % STG, src:src + w]).then_inc(z_v.sem, 1)
                pool.wait_ge(c_ld.sem, c_ld.at(0, 2))
                pool.wait_ge(z_te.sem, z_te.at(l, NZT))
                pool.sem_inc(waits_taken_pool, 1)

                def queries(to, q_of_pair):
                    for k in range(2):
                        last = nc.gpsimd.tensor_tensor(to[k], q_of_pair.rearrange("p o c -> p (o c)"),
                                                       const["half"][:, k:k + 1].to_broadcast([P, SEQ]), ALU.mult)
                    return last

                def dilated_pair(g):
                    nc.gpsimd.tensor_copy(p_k, kbT[:, ds(g, 1), :].rearrange("p o c -> p (o c)"))
                    queries(p_qd, qbT[:, ds(g, 1), :]).then_inc(a_q.sem, 1)

                queries(p_q, qaT[:, 0:1, :]).then_inc(a_q.sem, 1)
                pool.wait_ge(a_s.sem, a_s.at(l, 1))
                pool.wait_ge(sg_rdy.sem, sg_rdy.at(l, 3))
                pool.sem_inc(waits_taken_pool, 1)
                dilated_pair(0)
                with pool.Fori(0, ROUNDS - 1) as g:
                    pool.wait_ge(a_s.sem, a_s.at(l, g * STEPS + STEPS_A))
                    queries(p_q, qaT[:, ds(g + 1, 1), :]).then_inc(a_q.sem, 1)
                    pool.wait_ge(a_s.sem, a_s.at(l, g * STEPS + STEPS))
                    dilated_pair(g + 1)
                pool.wait_ge(og_k.sem, og_k.at(l, 8))
                pool.sem_inc(waits_taken_pool, 1)
                with pool.Fori(0, NB) as b:
                    it = l * NB + b
                    pool.wait_ge(sc_full.sem, sc_full.at(it, 0))
                    pool.wait_ge(sc_used.sem, sc_used.at(it, 0))
                    pool.sem_inc(waits_taken_pool, 1)
                    nc.gpsimd.memset(strips.rearrange("p a x -> p (a x)"), 0.0).then_inc(s_clear.sem, 1)
                    pool.wait_ge(s_clear.sem, s_clear.at(it, 1))
                    pool.sem_inc(waits_taken_pool, 1)
                    for a, block in ((0, 0), (0, 1), (0, 3), (1, 1), (1, 3), (2, 0)):
                        half = min(block, 1)
                        to = strips[:, a, :].rearrange("p (q x) -> p q x", q=4)[:, :, 0:P].rearrange(
                            "p q (g w) -> p q g w", g=4)[:, :, :, 8 * block:8 * block + 2]
                        nc.gpsimd.tensor_copy(to, qdb[:, :, ds(b, 1), 4 * half:4 * half + 4, :].rearrange(
                            "p q o t k -> p q (o t) k"))
                    nc.gpsimd.tensor_copy(q_s[:], qd[:, ds(b, 1), :].rearrange("p o r -> p (o r)")).then_inc(
                        s_q.sem, 1)
                    pool.wait_ge(td_full.sem, td_full.at(it, TD_SD + 1))
                    pool.wait_ge(s_mask.sem, s_mask.at(it, 1))
                    nc.gpsimd.tensor_tensor(
                        biasm.rearrange("p (j c) -> p j c", j=32), const["b_sel"][:].rearrange("p (j c) -> p j c", j=32),
                        stat[0:64, 32:64].unsqueeze(2).to_broadcast([64, 32, 64]), ALU.add).then_inc(s_bm.sem, 1)
                row_scale(l * 2 + 1)
                with pool.Fori(0, 8) as c:
                    for q in range(4):
                        f = c * 4 + q
                        v = uT[:, ds(f, 1), :].rearrange("p o t -> p (o t)")
                        pool.wait_ge(u_relu.sem, u_relu.at(l, f + 1))
                        nc.gpsimd.tensor_tensor(v, v, v, ALU.mult).then_inc(u_sq.sem, 1)
            row_scale(2 * DEPTH)

        @block.tensor
        def _(pe):
            begin(pe, "tensor")
            mm, tr = nc.tensor.matmul, nc.tensor.transpose

            def norm_transposes(r):
                for t in range(NT):
                    R = ROWS[t]
                    pe.wait_ge(xn_rdy.sem, xn_rdy.at(r, t + 1))
                    for half in range(2):
                        if t >= 2:
                            pe.wait_ge(h_rdy.sem, h_rdy.at(r, 2 * (t - 2) + half + 1))
                            pe.sem_inc(waits_taken_pe, 1)
                        B = bank[2 * (t % 2) + half]
                        for j in range(4):
                            k = half * 4 + j
                            last = tr(B[:, j * P:j * P + R], xn[0:R, t % 2, k * P:(k + 1) * P], ident[0:R, 0:R])
                        last.then_inc(n_tr.sem, 1)

            def rows_times_chunk(dst, t, n, width, start=True, stop=True):
                for k in range(KT):
                    last = mm(dst, hT[:, k, t * P:t * P + ROWS[t]], ring[:, n % 2, k * CH:k * CH + width],
                              start=start and k == 0, stop=stop and k == KT - 1)
                return last

            def z_transposes(l, n):
                kind, t = z_kind(n)
                if kind == "vb":
                    return
                R = ROWS[t]
                s, B = stg[0:R, n % STG, :], bank[6 + n % 2]
                pe.wait_ge(z_stg.sem, z_stg.at(l, n + 1))
                if n >= 2:
                    pe.wait_ge(z_te.sem, z_te.at(l, n - 1))
                    pe.sem_inc(waits_taken_pe, 1)
                first = {"cs": 256}.get(kind, 0)
                for j in range({"cs": 1, "wg": 1}.get(kind, 4)):
                    last = tr(B[:, j * P:j * P + R], s[:, first + j * P:first + (j + 1) * P], ident[0:R, 0:R])
                last.then_inc(z_tr.sem, 1)

            def project(l):
                pe.wait_ge(h_rdy.sem, h_rdy.at(l * 2, 2 * NT))
                for n in range(NZ + 1):
                    if n < NZ:
                        c, t = n // NT, n % NT
                        width = Z_CHUNKS[c][2] - Z_CHUNKS[c][1]
                        if t == 0:
                            w_arrived(l, c)
                        if n >= 2:
                            pe.wait_ge(z_stg.sem, z_stg.at(l, n - 1))
                        last = rows_times_chunk(bank[4 + n % 2][0:ROWS[t], 0:width], t, c, width)
                        last.then_inc(z_mm.sem, 1)
                    if n >= 1:
                        z_transposes(l, n - 1)

            def w_arrived(l, n):
                pe.wait_ge(w_ld[n % 2].sem, w_ld[n % 2].at(l, n // 2 + 1))

            def chunk_transposes(l, s):
                n = NCK_P
                for j in range(4):
                    u = 4 * s + j
                    pe.wait_ge(xt_p.sem, xt_p.at(l, max(u - 1, 0)))
                    pe.sem_inc(waits_taken_pe, 1)
                    for q in range(4):
                        k, pair = j // 2, (j % 2) * 4 + q
                        last = tr(bank[u % 2][:, q * n:(q + 1) * n],
                                  relaid[s][0:n, (k * 8 + pair) * P:(k * 8 + pair + 1) * P], ident[0:n, 0:n])
                    last.then_inc(ct_p.sem, 1)

            def prompt_hidden(l, s):
                n = NCK_P
                pe.wait_ge(xt_p.sem, xt_p.at(l, 4 * s + 4))
                out = bank[2 + s][:, 0:3 * n].rearrange("p (k n) -> p k n", k=3)
                for j in range(8):
                    mm(out, w1[:, s, j, :], xt[s][:, :, j, :], start=(j == 0), stop=False, skip_group_check=True)
                for j in range(8):
                    last = mm(out[:, :, 0:n - 1], w1[:, s, 8 + j, :], xt[s][:, :, j, 1:n], start=False, stop=(j == 7),
                              skip_group_check=True)
                last.then_inc(hid_p.sem, 1)

            def step_scores(l, g, m):
                n, w = g * STEPS + m, step_keys(m)
                if m < STEPS_A:
                    q, kT = p_q[a_step(m)[0]], (ktcp, ksT, kwT)[a_step(m)[1]]
                else:
                    q, kT = p_qd[(m - STEPS_A) // 4], p_k
                if m == 0:
                    pe.wait_ge(a_q.sem, a_q.at(l, 2 * g + 1))
                    pe.sem_inc(waits_taken_pe, 1)
                if m == STEPS_A:
                    pe.wait_ge(a_q.sem, a_q.at(l, 2 * g + 2))
                    pe.sem_inc(waits_taken_pe, 1)
                if not isinstance(n, int) or n >= 2:
                    pe.wait_ge(a_sb.sem, a_sb.at(l, n - 1))
                mm(bank[m % 2][:, 0:w], q[:, m % 4 * P:(m % 4 + 1) * P], kT[:, 0:w],
                   start=True, stop=True).then_inc(a_s.sem, 1)

            def step_transposes(l, g, m):
                n, w = g * STEPS + m, step_keys(m)
                pe.wait_ge(a_e.sem, a_e.at(l, n + 1))
                if not isinstance(n, int) or n >= 2:
                    pe.wait_ge(a_pt.sem, a_pt.at(l, n - 1))
                if w == NCK_P:
                    last = tr(bank[2 + m % 2][0:w, 0:P], p_sb[:, m % 4, 0:w], ident[:])
                else:
                    for c in range(w // P):
                        last = tr(bank[2 + m % 2][:, c * P:(c + 1) * P], p_sb[:, m % 4, c * P:(c + 1) * P], ident[:])
                last.then_inc(a_t.sem, 1)

            def step_outputs(l, g, m):
                n, w = g * STEPS + m, step_keys(m)
                pe.wait_ge(a_pt.sem, a_pt.at(l, n + 1))
                pe.wait_ge(a_acc.sem, a_acc.at(l, n - 1 if not isinstance(n, int) or n >= 1 else 0))
                dst, br = bank[4 + m % 2][:, 0:P], a_step(m)[1]
                if w == NCK_P:
                    last = mm(dst, p_pt[0:w, m % 2, 0:P], vcp[:], start=True, stop=True)
                else:
                    for c in range(w // P):
                        v = (vst[:, c, (br - 1) * P:br * P] if m < STEPS_A else
                             vst[:, c, ds(256 + g * P, P)])
                        last = mm(dst, p_pt[:, m % 2, c * P:(c + 1) * P], v, start=(c == 0), stop=(c == w // P - 1))
                last.then_inc(a_o.sem, 1)

            def pair_transposes(outputs, B):
                for t in range(4):
                    last = tr(B[:, t * P:(t + 1) * P], outputs[:, t, :], ident[:])
                last.then_inc(og_t.sem, 1)

            def prompt_steps(l, g, first, last, ends):
                for m in range(first, last):
                    if m < STEPS or not ends:
                        step_scores(l, *in_round(g, m))
                    if m >= 2 and (m - 2 < STEPS or not ends):
                        step_transposes(l, *in_round(g, m - 2))
                    if m >= 4:
                        step_outputs(l, g, m - 4)
                    if m == STEPS_A + 6:
                        pe.wait_ge(a_acc.sem, a_acc.at(l, g * STEPS + STEPS_A))
                        pe.wait_ge(og_k.sem, og_k.at(l, 2 * g))
                        pair_transposes(og, bank[6])
                    if m == STEPS + AHEAD - 1:
                        pe.wait_ge(a_acc.sem, a_acc.at(l, g * STEPS + STEPS))
                        pe.wait_ge(og_k.sem, og_k.at(l, 2 * g))
                        pair_transposes(ogd, bank[7])

            pe.wait_ge(first_ld.sem, first_ld.at(0, len(FIRST)))
            with pe.Fori(0, DEPTH) as l:
                norm_transposes(l * 2)
                project(l)
                pe.wait_ge(c_ld.sem, c_ld.at(0, 2))
                pe.wait_ge(raw_p.sem, raw_p.at(l, 4))
                for s in range(2):
                    chunk_transposes(l, s)
                pe.wait_ge(comp_ld.sem, comp_ld.at(l, 3))
                pe.wait_ge(z_te.sem, z_te.at(l, NZT))
                for s in range(2):
                    prompt_hidden(l, s)
                pe.wait_ge(hdone_p.sem, hdone_p.at(l, 1))
                for k in range(2):
                    last = mm(bank[4][64 * k:64 * k + 64, 0:NCK_P], w2[:, 0, :], hid[:, 0, k * NCK_P:(k + 1) * NCK_P],
                              start=True, stop=True)
                last.then_inc(kvc_p.sem, 1)
                pe.wait_ge(hdone_p.sem, hdone_p.at(l, 2))
                for k in range(2):
                    last = mm(bank[5][0:NCK_P, k * HD:(k + 1) * HD], hid[:, 1, k * NCK_P:(k + 1) * NCK_P], w2[:, 1, :],
                              start=True, stop=True)
                last.then_inc(kvc_p.sem, 1)
                pe.wait_ge(sg_rdy.sem, sg_rdy.at(l, 1))
                pe.sem_inc(waits_taken_pe, 1)
                mm(bank[6][0:64, 0:192], const["tsel"][:], gb, start=True, stop=True).then_inc(sg_mm.sem, 1)
                pe.wait_ge(kvc_pk.sem, kvc_pk.at(l, 2))
                pe.wait_ge(z_te.sem, z_te.at(l, NZT))
                pe.wait_ge(z_v.sem, z_v.at(l, 3 * NT))
                pe.wait_ge(sg_rdy.sem, sg_rdy.at(l, 2))
                pe.sem_inc(waits_taken_pe, 1)
                prompt_steps(l, 0, 0, AHEAD, False)
                with pe.Fori(0, ROUNDS - 1) as g:
                    prompt_steps(l, g, AHEAD, STEPS + AHEAD, False)
                prompt_steps(l, ROUNDS - 1, AHEAD, STEPS + AHEAD, True)

                with pe.Fori(0, NB) as b:
                    it = l * NB + b



                    pe.wait_ge(raw_ld.sem, raw_ld.at(it, NPG))
                    for s in range(2):
                        pe.wait_ge(sc_used.sem, sc_used.at(it, max(SC_HID + s - 3, 0)))
                        out = bank[2 + (SC_HID + s) % 4][:, 0:258].rearrange("p (k n) -> p k n", k=2)
                        for j in range(16):
                            first = 1 if j < 8 else 0
                            for k in range(2):
                                last = mm(out[:, k, first:first + P], w1[:, s, j, :], rawt[:, :, s, k, j % 8, :],
                                          start=(j == 0 and k == 0), stop=(j == 15 and k == 1), skip_group_check=True)
                        last.then_inc(sc_full.sem, 1)

                    pe.wait_ge(td_used.sem, td_used.at(it, 0))
                    pe.wait_ge(s_q.sem, s_q.at(it, 1))
                    pe.wait_ge(kda_ld.sem, kda_ld.at(it, 1))
                    S = bank[TD_SD % 2]

                    def dilated_scores(j):
                        tile = kdb[:, j - ND_A, :] if ND_A <= j < ND_A + 4 else kda[:, j % (ND_A + 4), :]
                        e, g = (0, 0) if j == 0 else (1, j - 1) if j < ND_A else (2, (j - ND_A) % 4)
                        late = j >= ND_A + 4
                        M, a = (P if e == 0 else 32), (0 if e < 2 else 1 if late else 2)
                        for p in range(4):
                            at = p * P + 32 * g
                            last = mm(S[32 * g:32 * g + M, e * P:(e + 1) * P], strips[:, a, at:at + M],
                                      tile[:, p * P:(p + 1) * P], start=(j == 0 and p == 0), stop=(late and p == 3),
                                      skip_group_check=True)
                        return last

                    for j in range(ND_A):
                        last = dilated_scores(j)
                    last.then_inc(kda_used.sem, 1)
                    pe.wait_ge(kdb_ld.sem, kdb_ld.at(it, 1))
                    for j in range(ND_A, ND_A + 4):
                        dilated_scores(j)
                    for p in range(4):
                        mm(S[:, 384:448], strips[:, 0, p * P:(p + 1) * P], knb[:, p, :], start=False, stop=(p == 3),
                           skip_group_check=True)

                    pe.wait_ge(sc_used.sem, sc_used.at(it, SC_HID + 2))
                    B = bank[2 + SC_KTC % 4]
                    for k in range(2):
                        last = mm(B[64 * k:64 * k + 64, 0:P], w2[:, 0, :], hid[:, 0, k * P:(k + 1) * P],
                                  start=True, stop=True)
                    last.then_inc(sc_full.sem, 1)
                    B = bank[2 + SC_VC % 4]
                    for k in range(2):
                        last = mm(B[:, k * HD:(k + 1) * HD], hid[:, 1, k * P:(k + 1) * P], w2[:, 1, :],
                                  start=(k == 0), stop=(k == 1), skip_group_check=True)
                    last.then_inc(sc_full.sem, 1)
                    q_a = q_s[:]
                    pe.wait_ge(win_ld.sem, win_ld.at(it, 1))
                    pe.wait_ge(sc_used.sem, sc_used.at(it, SC_KTC + 1))
                    mm(bank[2 + SC_S % 4][0:64, 0:P], q_a, ktc, start=True, stop=True).then_inc(sc_full.sem, 1)
                    mm(bank[2 + SC_WIN % 4][0:64, :], q_a, kw_sb[:, :, 0:128], start=True, stop=True).then_inc(
                        sc_full.sem, 1)
                    B = bank[2 + SC_NEW % 4]
                    pe.wait_ge(sc_used.sem, sc_used.at(it, SC_NEW - 3))
                    mm(B[0:64, 0:64], q_a, knw[:], start=True, stop=False, skip_group_check=True)
                    mm(B[0:64, 64:128], q_a, kns[:], start=False, stop=True, skip_group_check=True).then_inc(
                        sc_full.sem, 1)
                    pe.wait_ge(sc_used.sem, sc_used.at(it, max(SC_IMP - 3, 0)))
                    pe.sem_inc(waits_taken_pe, 1)
                    B = bank[2 + SC_IMP % 4]
                    pe.wait_ge(s_gs.sem, s_gs.at(it, 1))
                    pe.sem_inc(waits_taken_pe, 1)
                    mm(B[0:64, 0:P], gs[:], s_c, start=True, stop=True).then_inc(sc_full.sem, 1)
                    pe.wait_ge(kda_ld.sem, kda_ld.at(it, 2))
                    for j in range(ND_A + 4, ND_TILES):
                        last = dilated_scores(j)
                    last.then_inc(td_full.sem, 1)
                    pe.wait_ge(td_used.sem, td_used.at(it, max(TD_PTC - 1, 0)))
                    pe.sem_inc(waits_taken_pe, 1)
                    tr(bank[TD_PTC % 2][:, 0:64], s_c, ident[0:64, 0:64]).then_inc(td_full.sem, 1)
                    pe.wait_ge(sel_ld.sem, sel_ld.at(it, NPG))
                    for u in range(4):
                        pe.wait_ge(sc_used.sem, sc_used.at(it, max(SC_SEL + u - 3, 0)))
                        mm(bank[2 + (SC_SEL + u) % 4][0:64, :], q_a, kvsel[:, u * 4:u * 4 + 4, 0:128],
                           start=True, stop=True).then_inc(sc_full.sem, 1)
                    pe.wait_ge(s_exp.sem, s_exp.at(it, EX_WIN))
                    pe.wait_ge(td_used.sem, td_used.at(it, max(TD_PTW - 1, 0)))
                    pe.sem_inc(waits_taken_pe, 1)
                    B = bank[TD_PTW % 2]
                    for c in range(5):
                        R = P if c < 4 else 64
                        last = tr(B[0:R, c * 64:(c + 1) * 64], s_win[:, c * P:c * P + R], ident[0:64, 0:64])
                    last.then_inc(td_full.sem, 1)
                    pe.wait_ge(s_exp.sem, s_exp.at(it, EX_DIL))
                    pe.wait_ge(td_used.sem, td_used.at(it, max(TD_PTD - 1, 0)))
                    B = bank[TD_PTD % 2]
                    for e in range(4):
                        R = 64 if e == 3 else P
                        last = tr(B[0:R, e * P:(e + 1) * P], s_d[:, e * P:e * P + R], ident[:])
                    last.then_inc(td_full.sem, 1)
                    pe.wait_ge(vd_ld.sem, vd_ld.at(it, 1))
                    pe.wait_ge(td_used.sem, td_used.at(it, TD_PTD + 1))
                    for j in range(ND_TILES):
                        e, g = (0, 0) if j == 0 else (1, j - 1) if j < ND_A else (2, (j - ND_A) % 4)
                        late = j >= ND_A + 4
                        M = P if e == 0 else 8 if e == 2 and not late else 16
                        at = 32 * g + (16 if late else 0)
                        mm(bank[7][32 * g:32 * g + M, :], ptd[:, e, at:at + M], vd[:, j, :], start=(j == 0), stop=False,
                           skip_group_check=True)
                    mm(bank[7][:], ptd[0:64, 3, :], vsm[:, 256:768], start=False, stop=True,
                       skip_group_check=True).then_inc(od_full.sem, 1)
                    O = bank[6][:, 0:192].rearrange("p (e r) -> p e r", e=3)
                    mm(O[:, 0, :], vc, ptc, start=True, stop=False, skip_group_check=True)
                    for c in range(4):
                        mm(O[:, 2, :], kw_sb[:, c, 128:256], ptw[:, c, :], start=False, stop=False, skip_group_check=True)
                    mm(O[:, 2, :], vsm[:, 128:256], ptw[0:64, 4, :], start=False, stop=False,
                        skip_group_check=True).then_inc(win_pv.sem, 1)
                    pe.wait_ge(s_exp.sem, s_exp.at(it, EX_SEL))
                    for u in range(3):
                        pe.wait_ge(td_used.sem, td_used.at(it, max(TD_PTS + u - 1, 0)))
                        pe.sem_inc(waits_taken_pe, 1)
                        B = bank[(TD_PTS + u) % 2]
                        for c in range(u * 8, min(u * 8 + 8, 17)):
                            R = P if c < 16 else 64
                            last = tr(B[0:R, (c % 8) * 64:(c % 8 + 1) * 64], s_sel[:, c * P:c * P + R], ident[0:64, 0:64])
                        last.then_inc(td_full.sem, 1)
                    pe.wait_ge(td_used.sem, td_used.at(it, TD_PTS + 3))
                    for c in range(16):
                        mm(O[:, 1, :], kvsel[:, c, 128:256], pts[:, c, :], start=False, stop=False, skip_group_check=True)
                    mm(O[:, 1, :], vsm[:, 0:128], pts[0:64, 16, :], start=False, stop=True,
                        skip_group_check=True).then_inc(oa_full.sem, 1)
                    pe.wait_ge(d_scaled.sem, d_scaled.at(it, 1))
                    pe.wait_ge(sc_used.sem, sc_used.at(it, SC_DT - 3))
                    for p in range(4):
                        last = mm(bank[2 + SC_DT % 4][:, p * NS:(p + 1) * NS], d_own[:, p * P:(p + 1) * P],
                                  const["own_step"][:], start=(p == 0), stop=(p == 3), skip_group_check=True)
                    last.then_inc(sc_full.sem, 1)
                    pe.wait_ge(s_diag.sem, s_diag.at(it, 1))
                    pe.wait_ge(sc_used.sem, sc_used.at(it, max(SC_WBA - 3, 0)))
                    mm(bank[2 + SC_WBA % 4][:, 0:192], const["ones"][:], diag[:, 0:192], start=True, stop=True).then_inc(
                        sc_full.sem, 1)

                pe.wait_ge(out_put.sem, out_put.at(l * NB + NB - 1, 2))
                for half in range(2):
                    n = W_OUT0 + half
                    w_arrived(l, n)
                    for t in range(NT):
                        if half:
                            pe.wait_ge(y_add.sem, y_add.at(l, t + 1))
                        rows_times_chunk(bank[t][0:ROWS[t], :], t, n, CH).then_inc(y_mm.sem, 1)
                norm_transposes(l * 2 + 1)
                pe.wait_ge(h_rdy.sem, h_rdy.at(l * 2 + 1, 2 * NT))
                pe.sem_inc(waits_taken_pe, 1)
                with pe.Fori(0, 4) as c2:
                    for par in range(2):
                        n = W_UP0 + par
                        pe.wait_ge(w_ld[par].sem, w_ld[par].at(l, c2 + (n // 2 + 1)))
                        for q in range(4):
                            f = c2 * 8 + par * 4 + q
                            A, Bk = bank[2 * (q % 2)], bank[2 * (q % 2) + 1]
                            if q >= 2:
                                pe.wait_ge(u_relu.sem, u_relu.at(l, f - 1))
                            else:
                                pe.wait_ge(u_relu.sem, u_relu.at(l, c2 * 8 + par * 4))
                            for k in range(KT):
                                lhs = ring[:, par, k * CH + q * P:k * CH + (q + 1) * P]
                                mm(A[:, 0:TOK // 2], lhs, hT[:, k, 0:TOK // 2], start=(k == 0), stop=(k == KT - 1))
                                last = mm(Bk[:, 0:TOK // 2], lhs, hT[:, k, TOK // 2:TOK],
                                          start=(k == 0), stop=(k == KT - 1))
                            last.then_inc(u_mm.sem, 1)
                pe.wait_ge(u_sq.sem, u_sq.at(l, 32))
                for n in range(W_DN0, W_ALL):
                    half, c = (n - W_DN0) // 4, (n - W_DN0) % 4
                    w_arrived(l, n)
                    for t in range(NT):
                        if half and c == 0:
                            pe.wait_ge(d_add.sem, d_add.at(l, t + 1))
                        for k in range(8):
                            last = mm(bank[t][0:ROWS[t], :], uT[:, c * 8 + k, t * P:t * P + ROWS[t]],
                                      ring[:, n % 2, k * CH:(k + 1) * CH], start=(c == 0 and k == 0),
                                      stop=(c == 3 and k == 7))
                        if c == 3:
                            last.then_inc(d_mm.sem, 1)
                    if c < 3:
                        last.then_inc(d_chunk.sem, 1)

        @block.vector
        def _(dve):
            begin(dve, "vector")
            V = nc.vector

            class Order:

                def __init__(self, count, rnd, first=0):
                    self.sem, self.count, self.rnd, self.k, self.first = count.sem, count, rnd, 0, first

                def next(self):
                    self.k += 1
                    return self.count.at(self.rnd, self.first + self.k)

            def norm_keep(r, which):
                for t in range(NT):
                    R = ROWS[t]
                    for half in range(2):
                        dve.wait_ge(n_tr.sem, n_tr.at(r, 2 * t + half + 1))
                        V.tensor_tensor(
                            hT[:, half * 4:half * 4 + 4, t * P:t * P + R],
                            bank[2 * (t % 2) + half][:].rearrange("p (j c) -> p j c", j=4)[:, :, 0:R],
                            gain[:, which, half * 4:half * 4 + 4].unsqueeze(2).to_broadcast([P, 4, R]), ALU.mult).then_inc(
                                h_rdy.sem, 1)

            def z_keep(l, n):
                kind, t = z_kind(n)
                dve.wait_ge(z_tr.sem, z_tr.at(l, n + 1))
                B = bank[6 + n % 2]
                cols = slice(t * P, (t + 1) * P)
                by4 = B[:].rearrange("p (g c) -> p g c", g=4)
                if t < 4:
                    if kind in ("cs", "wg"):
                        last = V.tensor_copy((ksT if kind == "cs" else kwT)[:, cols], B[:, 0:P])
                    else:
                        last = V.tensor_copy({"qa": qaT, "qb": qbT, "kb": kbT}[kind][:, :, cols], by4)
                elif kind in ("cs", "wg"):
                    last = V.tensor_copy((kns if kind == "cs" else knw)[:], B[:, 0:64])
                elif kind == "kb":
                    last = V.tensor_copy(knb[:], by4[:, :, 0:64])
                else:
                    for k in range(2):
                        rows = slice(64 * k, 64 * k + 64)
                        if kind == "qa":
                            for g in range(4):
                                last = V.tensor_copy(qd[rows, :, 32 * k + 8 * g:32 * k + 8 * g + 8],
                                                     by4[rows, g, 0:64].rearrange("p (b t) -> p b t", b=NB))
                        else:
                            last = V.tensor_copy(qdb[rows, :, :, :, k].rearrange("p q b t -> p q (b t)"),
                                                 by4[rows, :, 0:64])
                last.then_inc(z_te.sem, 1)

            def hidden(order, n, s, src, done):
                V.tensor_scalar(he[:, 0:2 * n], he[:, 0:2 * n], 1.0, None, ALU.add).then_inc(order.sem, 1)
                dve.wait_ge(order.sem, order.next())
                V.reciprocal(he[:, 0:2 * n], he[:, 0:2 * n]).then_inc(order.sem, 1)
                dve.wait_ge(order.sem, order.next())
                V.scalar_tensor_tensor(hid[:, s, 0:2 * n], src[:, 0:2 * n], cbias[:, s:s + 1],
                                       he[:, 0:2 * n], ALU.add, ALU.mult).then_inc(done.sem, 1)

            def sparse_bias(g):
                for k in range(2):
                    slope = slopes[:, ds(8 * k + g * 2, 1)]
                    V.tensor_scalar(p_biasc[:, k, :], const["ndc"][:], slope, None, ALU.mult)
                    last = V.tensor_scalar(p_bias[:, k, :], const["nd"][:], slope, None, ALU.mult)
                last.then_inc(a_bias.sem, 1)

            def dilated_bias(g):
                for k in range(2):
                    last = V.scalar_tensor_tensor(p_biasd[:, k, :], const["nd"][:], slopes[:, ds(g * 4 + (2 * k + 1), 1)],
                                                  const["lnb"][:], ALU.mult, ALU.add)
                last.then_inc(a_bias.sem, 1)

            def step_bias(l, g, m):
                n, w, t = g * STEPS + m, step_keys(m), m % 4
                if m >= STEPS_A:
                    bias = p_biasd[:, (m - STEPS_A) // 4, SEQ - w:SEQ]
                elif w == NCK_P:
                    bias = p_biasc[:, m // 12, t * 32:(t + 1) * 32]
                else:
                    bias = p_bias[:, m // 12, SEQ - w:SEQ]
                if m == 0:
                    dve.wait_ge(a_bias.sem, a_bias.at(l, 2 * g + 1))
                if m == STEPS_A:
                    dve.wait_ge(a_bias.sem, a_bias.at(l, 2 * g + 2))
                if not isinstance(n, int) or n >= 4:
                    dve.wait_ge(a_t.sem, a_t.at(l, n - 3))
                dve.wait_ge(a_s.sem, a_s.at(l, n + 1))
                dve.sem_inc(waits_taken_dve, 1)
                V.tensor_tensor_reduce(p_sb[:, m % 4, 0:w], bank[m % 2][:, 0:w], bias, -1.0, BIG,
                                       ALU.add, ALU.min, stat[:, 16 + m % 4:17 + m % 4]).then_inc(a_sb.sem, 1)

            def step_add(l, g, m, order):
                t, k = m % 4, (m // 12 if m < STEPS_A else (m - STEPS_A) // 4)
                dve.wait_ge(a_o.sem, a_o.at(l, g * STEPS + m + 1))
                rc, w_ = sm[:, m % 4:m % 4 + 1], sm[:, 4 + m % 4:5 + m % 4]
                V.reciprocal(rc, stat[:, 32 + m % 8:33 + m % 8]).then_inc(order.sem, 1)
                dve.wait_ge(order.sem, order.next())
                src = bank[4 + m % 2][:, k * HD:(k + 1) * HD]
                if m >= STEPS_A:
                    last = V.tensor_scalar(ogd[:, t, k * HD:(k + 1) * HD], src, rc, None, ALU.mult)
                else:
                    dst, br = og[:, t, k * HD:(k + 1) * HD], a_step(m)[1]
                    gt = gate[:, t, ds(g * 3 + (12 * k + br), 1)]
                    if br == 0 and t == 0:
                        V.scalar_tensor_tensor(w_, rc, const["okrow"][:], gt, ALU.mult, ALU.mult).then_inc(order.sem, 1)
                    else:
                        V.tensor_tensor(w_, rc, gt, ALU.mult).then_inc(order.sem, 1)
                    dve.wait_ge(order.sem, order.next())
                    if br == 0:
                        last = V.tensor_scalar(dst, src, w_, None, ALU.mult)
                    else:
                        last = V.scalar_tensor_tensor(dst, src, w_, dst, ALU.mult, ALU.add)
                last.then_inc(a_acc.sem, 1)

            def prompt_steps(l, g, first, last, ends):
                order = Order(ch_a, l, g * (2 * STEPS_A + STEPS_D))
                for m in range(first, last):
                    if m < STEPS or not ends:
                        step_bias(l, *in_round(g, m))
                    if m == 4:
                        dve.wait_ge(a_sb.sem, a_sb.at(l, g * STEPS))
                        dilated_bias(g)
                    if m == STEPS_A + 1 and not ends:
                        dve.wait_ge(a_sb.sem, a_sb.at(l, g * STEPS + STEPS_A))
                        sparse_bias(g + 1)
                    if m == AHEAD:
                        dve.wait_ge(og_t.sem, og_t.at(l, 2 * g))
                    if m >= AHEAD:
                        step_add(l, g, m - AHEAD, order)
                    if m == STEPS_A + 7:
                        dve.wait_ge(og_t.sem, og_t.at(l, 2 * g + 1))
                        V.tensor_copy(hT[:, ds(g, 1), 0:SEQ].rearrange("p o c -> p (o c)"), bank[6][:]).then_inc(
                            og_k.sem, 1)
                dve.wait_ge(og_t.sem, og_t.at(l, 2 * g + 2))
                V.tensor_copy(hT[:, ds(g + 4, 1), 0:SEQ].rearrange("p o c -> p (o c)"), bank[7][:]).then_inc(
                    og_k.sem, 1)

            V.memset(stat[:], 1.0)
            V.memset(topk[:], 0.0)
            V.memset(qd[:], 0.0)
            V.memset(qdb[:], 0.0).then_inc(cleared.sem, 1)
            dve.wait_ge(cleared.sem, cleared.at(0, 1))
            dve.wait_ge(first_ld.sem, first_ld.at(0, len(FIRST)))
            with dve.Fori(0, DEPTH) as l:
                lay = Order(ch_l, l)
                dve.wait_ge(gain_ld.sem, gain_ld.at(l, 2))
                norm_keep(l * 2, 0)
                for n in range(NZT):
                    z_keep(l, n)
                dve.wait_ge(g_exp.sem, g_exp.at(l, NT))
                V.tensor_scalar(gate[:, 0:4, :], gate[:, 0:4, :], 1.0, None, ALU.add)
                V.tensor_scalar(gate[0:64, 4, :], gate[0:64, 4, :], 1.0, None, ALU.add).then_inc(g_rdy.sem, 1)
                dve.wait_ge(g_rdy.sem, g_rdy.at(l, 1))
                V.reciprocal(gate[:, 0:4, :], gate[:, 0:4, :])
                V.reciprocal(gate[0:64, 4, :], gate[0:64, 4, :]).then_inc(g_rdy.sem, 1)
                dve.wait_ge(g_rdy.sem, g_rdy.at(l, 2))
                dve.wait_ge(c_ld.sem, c_ld.at(0, 2))
                dve.wait_ge(comp_ld.sem, comp_ld.at(l, 3))
                for s in range(2):
                    V.memset(xt[s][:, 2], 0.0).then_inc(lay.sem, 1)
                    dve.wait_ge(lay.sem, lay.next())
                    V.tensor_copy(xt[s][:, 2, :, 0:2], pe_in[:, s, :].rearrange("p (h j) -> p j h", h=2))
                for s in range(2):
                    for j in range(4):
                        u = 4 * s + j
                        dve.wait_ge(ct_p.sem, ct_p.at(l, u + 1))
                        V.tensor_copy(xt[s][:, j // 2, j % 2 * 4:j % 2 * 4 + 4, :].rearrange("p j n -> p (j n)"),
                                      bank[u % 2][:, 0:4 * NCK_P]).then_inc(xt_p.sem, 1)
                for s in range(2):
                    dve.wait_ge(hid_p.sem, hid_p.at(l, s + 1))
                    V.tensor_copy(cbias[:, s:s + 1], bank[2 + s][:, 2 * NCK_P:2 * NCK_P + 1])
                    V.tensor_scalar(ncbias[:, s:s + 1], bank[2 + s][:, 2 * NCK_P:2 * NCK_P + 1], -1.0, None,
                                    ALU.mult).then_inc(pb_rdy.sem, 1)
                for s in range(2):
                    dve.wait_ge(hexp_p.sem, hexp_p.at(l, s + 1))
                    hidden(lay, NCK_P, s, bank[2 + s], hdone_p)
                V.tensor_tensor(
                    gb.rearrange("p (b e) -> p b e", b=NB), const["bsel"][:].unsqueeze(2).to_broadcast([64, NB, 24]),
                    gate[0:64, 4:5, :].to_broadcast([64, NB, 24]), ALU.mult).then_inc(sg_rdy.sem, 1)
                dve.wait_ge(kvc_p.sem, kvc_p.at(l, 1))
                V.tensor_copy(ktcp[:], bank[4][:, 0:NCK_P]).then_inc(kvc_pk.sem, 1)
                dve.wait_ge(kvc_p.sem, kvc_p.at(l, 2))
                V.tensor_copy(vcp[:], bank[5][0:NCK_P, 0:P]).then_inc(kvc_pk.sem, 1)
                dve.wait_ge(sg_mm.sem, sg_mm.at(l, 1))
                V.tensor_tensor(gm, bank[6][0:64, 0:192], const["hsel"][:], ALU.mult).then_inc(sg_rdy.sem, 1)
                dve.wait_ge(sg_rdy.sem, sg_rdy.at(l, 2))
                V.tensor_reduce(sgate[:], gm.rearrange("p (b h e) -> p b e h", b=NB, h=8), X, ALU.add).then_inc(
                    sg_rdy.sem, 1)
                dve.wait_ge(sg_rdy.sem, sg_rdy.at(l, 3))
                dve.sem_inc(waits_taken_dve, 1)

                sparse_bias(0)
                for m in range(AHEAD):
                    step_bias(l, 0, m)
                with dve.Fori(0, ROUNDS - 1) as g:
                    prompt_steps(l, g, AHEAD, STEPS + AHEAD, False)
                prompt_steps(l, ROUNDS - 1, AHEAD, STEPS + AHEAD, True)

                with dve.Fori(0, NB) as b:
                    it = l * NB + b
                    order = Order(ch_s, it)
                    new = ds(b * 64, 64)
                    put = ds(b * NS + SEQ, NS)
                    for s in range(2):
                        dve.wait_ge(s_hexp.sem, s_hexp.at(it, s + 1))
                        V.tensor_scalar(he, he, 1.0, None, ALU.add).then_inc(order.sem, 1)
                        dve.wait_ge(order.sem, order.next())
                        V.reciprocal(he, he).then_inc(order.sem, 1)
                        dve.wait_ge(order.sem, order.next())
                        V.scalar_tensor_tensor(
                            hid[:, s, :].rearrange("p (k n) -> p k n", k=2),
                            bank[2 + s][:, 0:258].rearrange("p (k n) -> p k n", k=2)[:, :, 1:129], cbias[:, s:s + 1],
                            he.rearrange("p (k n) -> p k n", k=2), ALU.add, ALU.mult).then_inc(sc_used.sem, 1)



                    def new_scores(dst, src, bias, least):
                        V.scalar_tensor_tensor(dst, src, -1.0, bias, ALU.mult, ALU.add).then_inc(order.sem, 1)
                        dve.wait_ge(order.sem, order.next())
                        return V.tensor_reduce(least, dst, X, ALU.min)

                    def negated(dst, src, bias, least):
                        return V.tensor_tensor_reduce(dst, src, bias, -1.0, BIG, ALU.add, ALU.min, least)

                    dve.wait_ge(sc_full.sem, sc_full.at(it, SC_KTC + 1))
                    V.tensor_copy(ktc, bank[2 + SC_KTC % 4][:, 0:P]).then_inc(sc_used.sem, 1)
                    dve.wait_ge(sc_full.sem, sc_full.at(it, SC_VC + 1))
                    dve.sem_inc(waits_taken_dve, 1)
                    V.tensor_copy(vc, bank[2 + SC_VC % 4][:, 0:P]).then_inc(sc_used.sem, 1)
                    dve.wait_ge(sc_full.sem, sc_full.at(it, SC_S + 1))
                    dve.sem_inc(waits_taken_dve, 1)
                    negated(s_c, bank[2 + SC_S % 4][0:64, 0:P], const["b_cmp"][:], stat[0:64, 24:25]).then_inc(
                        sc_used.sem, 1)
                    dve.wait_ge(sc_full.sem, sc_full.at(it, SC_WIN + 1))
                    dve.sem_inc(waits_taken_dve, 1)
                    negated(s_win[:, 0:WIN], bank[2 + SC_WIN % 4][0:64, :], const["b_win"][:], sm[0:64, 22:23]).then_inc(
                        sc_used.sem, 1)
                    dve.wait_ge(s_exp.sem, s_exp.at(it, EX_CMP))
                    V.reciprocal(sm[0:64, 8:9], stat[0:64, 28:29]).then_inc(order.sem, 1)
                    dve.wait_ge(order.sem, order.next())
                    V.tensor_scalar(gs[:], const["gsum"][:], sm[0:64, 8:9], None, ALU.mult).then_inc(s_gs.sem, 1)
                    dve.wait_ge(sc_full.sem, sc_full.at(it, SC_NEW + 1))
                    B = bank[2 + SC_NEW % 4]
                    new_scores(s_sel[:, PAST:PAST + 64], B[0:64, 64:128], const["nb_newa"][:, new], sm[0:64, 20:21])
                    new_scores(s_win[:, WIN:WIN + 64], B[0:64, 0:64], const["nb_newa"][:, new],
                               sm[0:64, 23:24]).then_inc(sc_used.sem, 1)
                    dve.wait_ge(sc_used.sem, sc_used.at(it, SC_NEW + 1))
                    V.tensor_reduce(stat[0:64, 25:26], sm[0:64, 22:24], X, ALU.min).then_inc(s_max.sem, 1)
                    dve.wait_ge(sc_full.sem, sc_full.at(it, SC_IMP + 1))
                    imp = bank[2 + SC_IMP % 4][0:64, 0:P].rearrange("p (j c) -> p j c", c=4)
                    sc_a, sc_b, sc_c, top = topk[:, 0:33], topk[:, 33:66], topk[:, 66:99], topk[:, 99:107]
                    V.tensor_reduce(sc_a[:, 0:32], imp, X, ALU.add).then_inc(order.sem, 1)
                    dve.wait_ge(order.sem, order.next())
                    V.tensor_tensor(sc_a[:, 1:32], sc_a[:, 1:32], imp[:, 0:31, 3], ALU.add).then_inc(sc_used.sem, 1)
                    dve.wait_ge(sc_used.sem, sc_used.at(it, SC_IMP + 1))
                    V.tensor_tensor(sc_b, sc_a, const["forced"][:], ALU.add).then_inc(order.sem, 1)
                    dve.wait_ge(order.sem, order.next())
                    dve.sem_inc(waits_taken_dve, 1)
                    V.max(top, sc_b).then_inc(order.sem, 1)
                    dve.wait_ge(order.sem, order.next())
                    dve.sem_inc(waits_taken_dve, 1)
                    V.match_replace(sc_c, top, sc_b, NEG).then_inc(order.sem, 1)
                    dve.wait_ge(order.sem, order.next())
                    dve.sem_inc(waits_taken_dve, 1)
                    V.max(top, sc_c).then_inc(order.sem, 1)
                    dve.wait_ge(order.sem, order.next())
                    dve.sem_inc(waits_taken_dve, 1)
                    V.match_replace(sc_b, top, sc_c, NEG).then_inc(order.sem, 1)
                    dve.wait_ge(order.sem, order.next())
                    V.tensor_scalar(stat[0:64, 32:64], sc_b[:, 0:32], NEG / 2, NEG, ALU.is_gt, ALU.mult).then_inc(
                        s_mask.sem, 1)
                    dve.wait_ge(td_full.sem, td_full.at(it, TD_SD + 1))
                    dve.sem_inc(waits_taken_dve, 1)
                    negated(s_d[:, 0:384], bank[TD_SD % 2][:, 0:384], const["b_dil"][:], sm[:, 24:25])
                    new_scores(s_d[:, 384:448], bank[TD_SD % 2][:, 384:448], const["nb_newd"][:, new],
                               sm[:, 25:26]).then_inc(order.sem, 1)
                    dve.wait_ge(order.sem, order.next())
                    V.tensor_reduce(stat[:, 26:27], sm[:, 24:26], X, ALU.min).then_inc(td_used.sem, 1)
                    dve.wait_ge(td_full.sem, td_full.at(it, TD_PTC + 1))
                    V.tensor_copy(ptc, bank[TD_PTC % 2][:, 0:64]).then_inc(td_used.sem, 1)
                    dve.wait_ge(td_full.sem, td_full.at(it, TD_PTW + 1))
                    B = bank[TD_PTW % 2]
                    V.tensor_copy(ptw[:, 0:4, :].rearrange("p c r -> p (c r)"), B[:, 0:256])
                    V.tensor_copy(ptw[0:64, 4, :], B[0:64, 256:320]).then_inc(td_used.sem, 1)
                    dve.wait_ge(td_full.sem, td_full.at(it, TD_PTD + 1))
                    B = bank[TD_PTD % 2]
                    V.tensor_copy(ptd[:, 0:3, :].rearrange("p e r -> p (e r)"), B[:, 0:384])
                    V.tensor_copy(ptd[0:64, 3, :], B[0:64, 384:512]).then_inc(td_used.sem, 1)
                    V.reciprocal(sm[:, 15:16], stat[:, 30:31]).then_inc(order.sem, 1)
                    dve.wait_ge(order.sem, order.next())
                    dve.wait_ge(s_bm.sem, s_bm.at(it, 1))
                    for u in range(4):
                        cols = slice(u * 512, (u + 1) * 512)
                        dve.wait_ge(sc_full.sem, sc_full.at(it, SC_SEL + u + 1))
                        dve.sem_inc(waits_taken_dve, 1)
                        negated(s_sel[:, cols], bank[2 + (SC_SEL + u) % 4][0:64, :], biasm[:, cols],
                                sm[0:64, 16 + u:17 + u]).then_inc(sc_used.sem, 1)
                    dve.wait_ge(sc_used.sem, sc_used.at(it, SC_SEL + 4))
                    V.tensor_reduce(stat[0:64, 27:28], sm[0:64, 16:21], X, ALU.min).then_inc(s_max.sem, 1)
                    dve.wait_ge(od_full.sem, od_full.at(it, 1))
                    V.scalar_tensor_tensor(
                        d_own.rearrange("p (h d) -> p h d", h=8), bank[7][:].rearrange("p (h d) -> p h d", h=8),
                        sm[:, 15:16], const["own_head"][:].unsqueeze(2).to_broadcast([P, 8, HD]),
                        ALU.mult, ALU.mult).then_inc(d_scaled.sem, 1)
                    for u in range(3):
                        dve.wait_ge(td_full.sem, td_full.at(it, TD_PTS + u + 1))
                        B = bank[(TD_PTS + u) % 2]
                        if u < 2:
                            last = V.tensor_copy(pts[:, 8 * u:8 * u + 8, :].rearrange("p c r -> p (c r)"), B[:])
                        else:
                            last = V.tensor_copy(pts[0:64, 16, :], B[0:64, 0:64])
                        last.then_inc(td_used.sem, 1)
                    dve.wait_ge(s_exp.sem, s_exp.at(it, EX_SEL))
                    V.reciprocal(sm[0:64, 9:13], stat[0:64, 28:32]).then_inc(order.sem, 1)
                    dve.wait_ge(order.sem, order.next())
                    V.tensor_tensor(sm[0:64, 26:27], sm[0:64, 9:10], sgate[:, ds(b, 1), 0], ALU.mult).then_inc(
                        order.sem, 1)
                    dve.wait_ge(order.sem, order.next())
                    V.tensor_tensor(sm[0:64, 27:28], sm[0:64, 12:13], sgate[:, ds(b, 1), 1], ALU.mult)
                    V.tensor_tensor(sm[0:64, 28:29], sm[0:64, 10:11], sgate[:, ds(b, 1), 2], ALU.mult).then_inc(
                        order.sem, 1)
                    dve.wait_ge(order.sem, order.next())
                    V.tensor_tensor(
                        diag[:, 0:192].rearrange("p (e r) -> p e r", e=3),
                        ident[0:64, 0:64].unsqueeze(1).to_broadcast([64, 3, 64]),
                        sm[0:64, 26:29].unsqueeze(2).to_broadcast([64, 3, 64]), ALU.mult).then_inc(s_diag.sem, 1)
                    dve.wait_ge(sc_full.sem, sc_full.at(it, SC_DT + 1))
                    V.tensor_copy(hT[:, 4:8, put],
                                  bank[2 + SC_DT % 4][:, 0:4 * NS].rearrange("p (q t) -> p q t", q=4)).then_inc(
                        sc_used.sem, 1)
                    dve.wait_ge(sc_full.sem, sc_full.at(it, SC_WBA + 1))
                    V.tensor_copy(wb[:, 0:192], bank[2 + SC_WBA % 4][:, 0:192]).then_inc(sc_used.sem, 1)
                    dve.wait_ge(sc_used.sem, sc_used.at(it, SC_WBA + 1))
                    dve.wait_ge(oa_full.sem, oa_full.at(it, 1))
                    V.tensor_tensor(prod, bank[6][:, 0:192], wb[:, 0:192], ALU.mult).then_inc(order.sem, 1)
                    dve.wait_ge(order.sem, order.next())
                    for k in range(2):
                        rows = slice(64 * k, 64 * k + 64)
                        V.tensor_reduce(
                            hT[rows, 0:4, put], prod[rows, :].rearrange("p (e k g t) -> p k g t e", e=3, k=2, g=4)[:, k],
                            X, ALU.add).then_inc(out_put.sem, 1)
                if order.k != CH_S or lay.k != CH_L:
                    raise ValueError((order.k, lay.k))

                for n in range(2 * NT):
                    half, t = n // NT, n % NT
                    v = x[0:ROWS[t], t, half * CH:(half + 1) * CH]
                    dve.wait_ge(y_mm.sem, y_mm.at(l, n + 1))
                    V.tensor_tensor(v, v, bank[t][0:ROWS[t], :], ALU.add).then_inc(y_add.sem, 1)
                norm_keep(l * 2 + 1, 1)
                for n in range(2 * NT):
                    half, t = n // NT, n % NT
                    v = x[0:ROWS[t], t, half * CH:(half + 1) * CH]
                    dve.wait_ge(d_mm.sem, d_mm.at(l, n + 1))
                    V.tensor_tensor(v, v, bank[t][0:ROWS[t], :], ALU.add).then_inc(d_add.sem, 1)
            dve.wait_ge(rstd.sem, rstd.at(2 * DEPTH, 2))
            dve.wait_ge(gfin_ld.sem, gfin_ld.at(0, 1))
            for t in range(NT):
                R = ROWS[t]
                V.scalar_tensor_tensor(x[0:R, t, :], x[0:R, t, :], stat[0:R, 8 + t:9 + t], gfin[0:R, :],
                                       ALU.mult, ALU.mult).then_inc(fin.sem, 1)


def laid_out(inputs):
    a = {n: np.asarray(v) for n, v in inputs.items()}
    put = {n: a[n] for n in ("x_prompt", "x_sample", "page_table", "w_in", "w_up", "w_down", "norm_final")}
    for n in ("norm_attn", "norm_mlp"):
        put[n] = a[n].reshape(DEPTH, KT, P).transpose(0, 2, 1)
    put["cmp_pe"] = a["cmp_pe"].reshape(DEPTH, 2, 16, 2, HD).transpose(0, 3, 4, 1, 2).reshape(DEPTH, P, 32)
    put["cmp_w1"] = a["cmp_w1"].reshape(DEPTH, 2, 16, 2, HD, 128).transpose(0, 3, 4, 1, 2, 5).reshape(DEPTH, P, -1)
    put["cmp_w2"] = a["cmp_w2"].transpose(0, 2, 1, 3).reshape(DEPTH, P, -1)
    w = a["w_out"]
    sparse = w[:, 0:512].reshape(DEPTH, 2, 4, HD, D).transpose(0, 2, 1, 3, 4).reshape(DEPTH, 512, D)
    put["w_out"] = np.concatenate([sparse, w[:, 512:]], 1)
    put["cache_kv_cmp"] = a["cache_kv_cmp"].reshape(DEPTH, POOL, 8, 8, 2, 2, 2, HD).transpose(
        0, 1, 4, 7, 5, 6, 3, 2).reshape(DEPTH, POOL, P, 256)

    def kt_and_v(rows):
        k, v = rows[..., 0, :, :], rows[..., 1, :, :]
        k = k.reshape(k.shape[:-2] + (P,))
        v = v.reshape(v.shape[:-2] + (P,))
        return np.concatenate([np.swapaxes(k, -1, -2), v], -1)

    put["cache_kv_sel"] = kt_and_v(a["cache_kv_sel"])
    win = a["state_kv_win"]
    put["window_tiles"] = kt_and_v(win.reshape(DEPTH, NB, 4, P, 2, 2, HD)).transpose(0, 1, 3, 2, 4)
    put["state_kv_win"] = win.reshape(DEPTH, NB, WIN, 256)
    dil = a["state_kv_dil"]
    put["state_kv_dil"] = dil.reshape(DEPTH, NB, PAST, D)
    by4 = dil[:, :, PAST - 4 * P:].reshape(DEPTH, NB, P, 4, 2, 8, HD)
    by16 = dil.reshape(DEPTH, NB, P, 16, 2, 8, HD)[:, :, :, 0:8]
    tiles = np.concatenate([dil[:, :, PAST - P:, None], by4, by16], 3)
    put["dilated_v"] = tiles[..., 1, :, :].reshape(DEPTH, NB, P, ND_TILES, CH)
    put["dilated_k"] = tiles[..., 0, :, :].reshape(DEPTH, NB, P, ND_TILES, 4, 2, HD).transpose(
        0, 1, 5, 6, 3, 4, 2).reshape(DEPTH, NB, P, ND_TILES, CH)
    return {n: np.ascontiguousarray(v) for n, v in put.items()}


OUT_SHAPES = {
    "y_p": (1, SEQ, D), "y_s": (NB, NS, D), "cmp_p": (DEPTH, 1, SEQ, 256), "sel_p": (DEPTH, 1, SEQ, 256),
    "win_p": (DEPTH, 1, SEQ, 256), "dil_p": (DEPTH, 1, SEQ, 1024), "cmp_s": (DEPTH, NB, NS, 256),
    "sel_s": (DEPTH, NB, NS, 256), "win_s": (DEPTH, NB, WIN, 256), "dil_s": (DEPTH, NB, PAST, 1024)}


def kernel(**inputs):
    import concourse.bacc as bacc
    from concourse.bass_utils import run_bass_kernel_spmd

    nc = bacc.Bacc("TRN2", target_bir_lowering=False, num_devices=1)
    arrays = laid_out(inputs)
    arrays.update(shape_constants())
    i = {n: nc.dram_tensor(f"in_{n}", a.shape, mybir.dt.from_np(a.dtype), kind="ExternalInput").ap()
         for n, a in arrays.items()}
    o = {n: nc.dram_tensor(f"out_{n}", shape, F32, kind="ExternalOutput").ap() for n, shape in OUT_SHAPES.items()}
    build(nc, i, o)
    r = run_bass_kernel_spmd(nc, [{f"in_{n}": a for n, a in arrays.items()}], core_ids=[0]).results[0]
    got = []
    for n, shape in OUT_SHAPES.items():
        heads = {"cmp": 2, "sel": 2, "win": 2, "dil": 8}.get(n[:3])
        a = r[f"out_{n}"]
        got.append(a.reshape(shape[:-1] + (2, heads, HD)) if heads else a)
    return tuple(got)
```
